# Optimizing a Trainium2 kernel written in Bass

```python
import math
import jax
import jax.numpy as jnp
from jax import lax
import numpy as np

D_MODEL = 1024
BATCH = 1
SEQ = 512
DEPTH = 2

HEAD_DIM = 64
ATTN_HQ = 8
ATTN_HKV = 2
ATTN_GROUP = ATTN_HQ // ATTN_HKV
WINDOW = 128
ATTN_BLOCK = 128
ROT_DIM = HEAD_DIM // 4
ROPE_THETA = 500000.0
DN_H = 4
DN_DK = 64
DN_DV = 64
DN_CONV = 4
DN_CHUNK = 64
CV_GROUPS = 4
CV_C = CV_GROUPS * HEAD_DIM
CV_K = 31
ATTN_QW = ATTN_HQ * HEAD_DIM
ATTN_KVW = ATTN_HKV * HEAD_DIM
DN_KW = DN_H * DN_DK
DN_VW = DN_H * DN_DV
D_MIX = ATTN_QW + DN_VW + CV_C
IN_SIZES = (ATTN_QW, ATTN_KVW, ATTN_KVW, DN_KW, DN_KW, DN_VW, DN_H, DN_H, DN_VW, 2 * CV_C)
N_IN = ATTN_QW + 2 * ATTN_KVW + 2 * DN_KW + 2 * DN_VW + 2 * DN_H + 2 * CV_C
D_FF = 2816
N_EXPERTS = 8
TOP_K = 2
D_FF_EXPERT = 1024
N_DENSE = (DEPTH + 1) // 2
N_MOE = DEPTH // 2
EPS = 1e-6

kernel_name = 'hymba_style_swa_deltanet_conformer_moe_adaln'

def rmsnorm(x, g):
    xf = x.astype(jnp.float32)
    y = xf * lax.rsqrt(jnp.mean(xf * xf, axis=-1, keepdims=True) + EPS)
    return (y * g.astype(jnp.float32)).astype(x.dtype)

def layernorm(x, g, b):
    xf = x.astype(jnp.float32)
    mu = jnp.mean(xf, axis=-1, keepdims=True)
    xc = xf - mu
    y = xc * lax.rsqrt(jnp.mean(xc * xc, axis=-1, keepdims=True) + EPS)
    return (y * g.astype(jnp.float32) + b.astype(jnp.float32)).astype(x.dtype)

def l2norm(x):
    return x * lax.rsqrt(jnp.sum(x * x, axis=-1, keepdims=True) + EPS)

def causal_dwconv(x, w):
    K, C = w.shape
    return lax.conv_general_dilated(x, w[:, None, :].astype(x.dtype), window_strides=(1,), padding=[(K - 1, 0)],
                                    dimension_numbers=('NWC', 'WIO', 'NWC'), feature_group_count=C)

def partial_rope(x, cos, sin):
    half = ROT_DIM // 2
    x1 = x[..., :half].astype(jnp.float32)
    x2 = x[..., half:ROT_DIM].astype(jnp.float32)
    r1 = (x1 * cos - x2 * sin).astype(x.dtype)
    r2 = (x2 * cos + x1 * sin).astype(x.dtype)
    return jnp.concatenate([r1, r2, x[..., ROT_DIM:]], axis=-1)

def swa_attention(q, k, v, sinks):
    B, S = q.shape[0], q.shape[1]
    NB = S // ATTN_BLOCK
    qb = q.reshape(B, NB, ATTN_BLOCK, ATTN_HKV, ATTN_GROUP, HEAD_DIM)

    def band(t):
        tp = jnp.pad(t, ((0, 0), (ATTN_BLOCK, 0), (0, 0), (0, 0)))
        tb = tp.reshape(B, NB + 1, ATTN_BLOCK, ATTN_HKV, HEAD_DIM)
        return jnp.concatenate([tb[:, :-1], tb[:, 1:]], axis=2)

    kb, vb = band(k), band(v)
    s = jnp.einsum('bnqhgd,bnkhd->bnhgqk', qb, kb, preferred_element_type=jnp.float32) * (HEAD_DIM ** -0.5)
    qi = jnp.arange(ATTN_BLOCK)[:, None]
    kj = jnp.arange(2 * ATTN_BLOCK)[None, :]
    diff = qi + ATTN_BLOCK - kj
    band_ok = (diff >= 0) & (diff < WINDOW)
    key_pos = jnp.arange(NB)[:, None] * ATTN_BLOCK - ATTN_BLOCK + kj
    valid = band_ok[None] & (key_pos >= 0)[:, None, :]
    s = jnp.where(valid[None, :, None, None], s, -jnp.inf)
    sink = sinks.astype(jnp.float32).reshape(1, 1, ATTN_HKV, ATTN_GROUP, 1, 1)
    m = jnp.maximum(jnp.max(s, axis=-1, keepdims=True), sink)
    p = jnp.exp(s - m)
    p = p / (jnp.sum(p, axis=-1, keepdims=True) + jnp.exp(sink - m))
    o = jnp.einsum('bnhgqk,bnkhd->bnqhgd', p.astype(v.dtype), vb)
    return o.reshape(B, S, ATTN_QW)

def gated_delta_rule(q, k, v, g, beta):
    B, S, H, DK = q.shape
    DV = v.shape[-1]
    C = DN_CHUNK
    N = S // C
    q = q * (DK ** -0.5)

    def chunk(t):
        return t.reshape(B, N, C, H, t.shape[-1]).transpose(0, 3, 1, 2, 4)

    qc, kc, vc = chunk(q), chunk(k), chunk(v)
    gc = jnp.cumsum(g.reshape(B, N, C, H).transpose(0, 3, 1, 2), axis=-1)
    bc = beta.reshape(B, N, C, H).transpose(0, 3, 1, 2)
    tril_incl = jnp.tril(jnp.ones((C, C), dtype=bool))
    strict = jnp.tril(jnp.ones((C, C), dtype=bool), -1)
    decay = jnp.exp(jnp.where(tril_incl, gc[..., :, None] - gc[..., None, :], -jnp.inf))
    kbeta = kc * bc[..., None]
    L = jnp.where(strict, jnp.einsum('bhnid,bhnjd->bhnij', kbeta, kc) * decay, 0.0)
    eye = jnp.eye(C, dtype=jnp.float32)
    T = lax.linalg.triangular_solve(eye + L, jnp.broadcast_to(eye, L.shape), left_side=True, lower=True,
                                    unit_diagonal=True)
    u = jnp.einsum('bhnij,bhnjd->bhnid', T, vc * bc[..., None])
    w = jnp.einsum('bhnij,bhnjd->bhnid', T, kbeta * jnp.exp(gc)[..., None])
    a_intra = jnp.einsum('bhnid,bhnjd->bhnij', qc, kc) * decay
    qg = qc * jnp.exp(gc)[..., None]
    kg = kc * jnp.exp(gc[..., -1:] - gc)[..., None]
    glast = jnp.exp(gc[..., -1])

    def step(state, inp):
        q_i, k_i, u_i, w_i, a_i, gl = inp
        v_new = u_i - jnp.einsum('bhck,bhkv->bhcv', w_i, state)
        o = jnp.einsum('bhck,bhkv->bhcv', q_i, state) + jnp.einsum('bhij,bhjv->bhiv', a_i, v_new)
        state = state * gl[..., None, None] + jnp.einsum('bhck,bhcv->bhkv', k_i, v_new)
        return state, o

    xs = tuple(jnp.moveaxis(t, 2, 0) for t in (qg, kg, u, w, a_intra, glast))
    s0 = jnp.zeros((B, H, DK, DV), jnp.float32)
    _, o = lax.scan(step, s0, xs)
    o = jnp.moveaxis(o, 0, 2).transpose(0, 2, 3, 1, 4)
    return o.reshape(B, S, H, DV)

def token_mixer(h, cos, sin, w_in, sinks, dn_conv_w, dn_a_log, dn_dt_bias, dn_norm_g,
                cv_dw_w, cv_dw_b, cv_ln_g, cv_ln_b, w_out):
    B, S, _ = h.shape
    f32 = jnp.float32
    proj = h @ w_in
    idx = np.cumsum(IN_SIZES)[:-1].tolist()
    aq, ak, av, dq, dk, dv, db, da, dz, cv = jnp.split(proj, idx, axis=-1)

    q = partial_rope(aq.reshape(B, S, ATTN_HQ, HEAD_DIM), cos, sin)
    k = partial_rope(ak.reshape(B, S, ATTN_HKV, HEAD_DIM), cos, sin)
    v = av.reshape(B, S, ATTN_HKV, HEAD_DIM)
    y_attn = swa_attention(q, k, v, sinks)

    qkv = jax.nn.silu(causal_dwconv(jnp.concatenate([dq, dk, dv], axis=-1), dn_conv_w))
    dq, dk, dv = jnp.split(qkv, [DN_KW, 2 * DN_KW], axis=-1)
    qd = l2norm(dq.reshape(B, S, DN_H, DN_DK).astype(f32))
    kd = l2norm(dk.reshape(B, S, DN_H, DN_DK).astype(f32))
    vd = dv.reshape(B, S, DN_H, DN_DV).astype(f32)
    beta = jax.nn.sigmoid(db.astype(f32))
    g = -jnp.exp(dn_a_log.astype(f32)) * jax.nn.softplus(da.astype(f32) + dn_dt_bias.astype(f32))
    o = gated_delta_rule(qd, kd, vd, g, beta)
    o = o * lax.rsqrt(jnp.mean(o * o, axis=-1, keepdims=True) + EPS) * dn_norm_g.astype(f32)
    o = o * jax.nn.silu(dz.reshape(B, S, DN_H, DN_DV).astype(f32))
    y_dn = o.reshape(B, S, DN_VW).astype(h.dtype)

    ca, cb = jnp.split(cv, 2, axis=-1)
    u = ca * jax.nn.sigmoid(cb)
    u = causal_dwconv(u, cv_dw_w) + cv_dw_b
    y_cv = jax.nn.silu(layernorm(u, cv_ln_g, cv_ln_b))

    return jnp.concatenate([y_attn, y_dn, y_cv], axis=-1) @ w_out

def swiglu(h, w_gate, w_up, w_down):
    return (jax.nn.silu(h @ w_gate) * (h @ w_up)) @ w_down

def moe_ffn(h, router_w, router_b, w_gate, w_up, w_down):
    B, S, D = h.shape
    t = h.reshape(B * S, D)
    logits = (t @ router_w).astype(jnp.float32) + router_b.astype(jnp.float32)
    top_v, top_i = lax.top_k(logits, TOP_K)
    top_p = jax.nn.softmax(top_v, axis=-1)
    combine = jnp.sum(jax.nn.one_hot(top_i, N_EXPERTS, dtype=jnp.float32) * top_p[..., None], axis=1)
    out = jnp.zeros_like(t)
    for e in range(N_EXPERTS):
        out = out + combine[:, e:e + 1].astype(t.dtype) * swiglu(t, w_gate[e], w_up[e], w_down[e])
    return out.reshape(B, S, D)

def modulate(x, g, shift, scale):
    return rmsnorm(x, g) * (1.0 + scale[:, None, :]) + shift[:, None, :]

def setup_inputs(seed: int = 0) -> dict:
    key = jax.random.key(seed)
    ks = jax.random.split(key, 32)
    f32 = jnp.float32

    def nrm(k, shape, s):
        return jax.random.normal(k, shape, f32) * s

    def gain(k, shape):
        return 1.0 + 0.02 * jax.random.normal(k, shape, f32)

    dt = jnp.exp(jax.random.uniform(ks[10], (DEPTH, DN_H), f32, math.log(1e-3), math.log(1e-1)))
    return {
        'x': nrm(ks[0], (BATCH, SEQ, D_MODEL), 1.0),
        'c': nrm(ks[1], (BATCH, D_MODEL), 1.0),
        'positions': jnp.broadcast_to(jnp.arange(SEQ, dtype=jnp.int32), (BATCH, SEQ)),
        'ada_w': nrm(ks[2], (DEPTH, 2, D_MODEL, 3 * D_MODEL), D_MODEL ** -0.5),
        'ada_b': nrm(ks[3], (DEPTH, 2, 3 * D_MODEL), 0.01),
        'norm_mix_g': gain(ks[4], (DEPTH, D_MODEL)),
        'norm_ffn_g': gain(ks[5], (DEPTH, D_MODEL)),
        'w_in': nrm(ks[6], (DEPTH, D_MODEL, N_IN), D_MODEL ** -0.5),
        'attn_sinks': nrm(ks[7], (DEPTH, ATTN_HQ), 0.5),
        'dn_conv_w': nrm(ks[8], (DEPTH, DN_CONV, 2 * DN_KW + DN_VW), DN_CONV ** -0.5),
        'dn_a_log': jnp.log(jax.random.uniform(ks[9], (DEPTH, DN_H), f32, 1.0, 16.0)),
        'dn_dt_bias': jnp.log(jnp.expm1(dt)),
        'dn_norm_g': gain(ks[11], (DEPTH, DN_DV)),
        'cv_dw_w': nrm(ks[12], (DEPTH, CV_K, CV_C), CV_K ** -0.5),
        'cv_dw_b': nrm(ks[13], (DEPTH, CV_C), 0.01),
        'cv_ln_g': gain(ks[14], (DEPTH, CV_C)),
        'cv_ln_b': nrm(ks[15], (DEPTH, CV_C), 0.01),
        'w_out': nrm(ks[16], (DEPTH, D_MIX, D_MODEL), D_MIX ** -0.5),
        'ffn_w_gate': nrm(ks[17], (N_DENSE, D_MODEL, D_FF), D_MODEL ** -0.5),
        'ffn_w_up': nrm(ks[18], (N_DENSE, D_MODEL, D_FF), D_MODEL ** -0.5),
        'ffn_w_down': nrm(ks[19], (N_DENSE, D_FF, D_MODEL), D_FF ** -0.5),
        'router_w': nrm(ks[20], (N_MOE, D_MODEL, N_EXPERTS), D_MODEL ** -0.5),
        'router_b': nrm(ks[21], (N_MOE, N_EXPERTS), 0.01),
        'moe_w_gate': nrm(ks[22], (N_MOE, N_EXPERTS, D_MODEL, D_FF_EXPERT), D_MODEL ** -0.5),
        'moe_w_up': nrm(ks[23], (N_MOE, N_EXPERTS, D_MODEL, D_FF_EXPERT), D_MODEL ** -0.5),
        'moe_w_down': nrm(ks[24], (N_MOE, N_EXPERTS, D_FF_EXPERT, D_MODEL), D_FF_EXPERT ** -0.5),
        'final_norm_g': gain(ks[25], (D_MODEL,)),
    }

def reference(x, c, positions, ada_w, ada_b, norm_mix_g, norm_ffn_g, w_in, attn_sinks, dn_conv_w, dn_a_log,
              dn_dt_bias, dn_norm_g, cv_dw_w, cv_dw_b, cv_ln_g, cv_ln_b, w_out, ffn_w_gate, ffn_w_up, ffn_w_down,
              router_w, router_b, moe_w_gate, moe_w_up, moe_w_down, final_norm_g):
    inv_freq = ROPE_THETA ** (-jnp.arange(0, ROT_DIM, 2, dtype=jnp.float32) / ROT_DIM)
    ang = positions.astype(jnp.float32)[..., None] * inv_freq
    cos = jnp.cos(ang)[:, :, None, :]
    sin = jnp.sin(ang)[:, :, None, :]
    c_act = jax.nn.silu(c)
    for l in range(DEPTH):
        mod = jnp.einsum('bd,kde->kbe', c_act, ada_w[l]) + ada_b[l][:, None, :]
        sh1, sc1, gt1 = jnp.split(mod[0], 3, axis=-1)
        sh2, sc2, gt2 = jnp.split(mod[1], 3, axis=-1)
        h = modulate(x, norm_mix_g[l], sh1, sc1)
        y = token_mixer(h, cos, sin, w_in[l], attn_sinks[l], dn_conv_w[l], dn_a_log[l], dn_dt_bias[l],
                        dn_norm_g[l], cv_dw_w[l], cv_dw_b[l], cv_ln_g[l], cv_ln_b[l], w_out[l])
        x = x + gt1[:, None, :] * y
        h = modulate(x, norm_ffn_g[l], sh2, sc2)
        if l % 2 == 0:
            j = l // 2
            f = swiglu(h, ffn_w_gate[j], ffn_w_up[j], ffn_w_down[j])
        else:
            j = l // 2
            f = moe_ffn(h, router_w[j], router_b[j], moe_w_gate[j], moe_w_up[j], moe_w_down[j])
        x = x + gt2[:, None, :] * f
    return rmsnorm(x, final_norm_g)


_drawn_inputs = setup_inputs


def setup_inputs(seed=0):
    import zlib

    import numpy as np

    out = dict(_drawn_inputs(seed))
    spreads = {}
    factors = {'attn_sinks': 24.516,
     'dn_norm_g': 14.619,
     'cv_dw_b': 5.292,
     'cv_ln_g': 8.277,
     'cv_ln_b': 36.106,
     'router_b': 32.625,
     'final_norm_g': 22.041,
     'norm_ffn_g': 3.161}
    for name, (base, spread) in spreads.items():
        noise = np.random.default_rng([zlib.crc32(name.encode()), seed]).standard_normal(out[name].shape)
        drawn = base * np.exp(spread * noise) if base else spread * noise
        out[name] = jnp.asarray(drawn.astype(out[name].dtype))
    for name, factor in factors.items():
        out[name] = (out[name] * factor).astype(out[name].dtype)
    return out
```

```python
import numpy as np

import concourse.bass as bass
from concourse import mybir
from contextlib import ExitStack

F32 = mybir.dt.float32
F32R = mybir.dt.float32r
I32 = mybir.dt.int32
ALU = mybir.AluOpType
ACT = mybir.ActivationFunctionType
AX = mybir.AxisListType

P = 128
D = 1024
S = 512
DC = D // P
DEPTH = 2
HD = 64
HQ, HKV = 8, 2
ROT = HD // 4
DN_CONV, DN_CHUNK = 4, 64
NCH = S // DN_CHUNK
NU = 2 * NCH
CV_K = 31
D_FF = 2816
FC = D_FF // P
NE = 8
FE = 1024 // P
N_IN_TILES = 18
EPS = 1e-6
NEG = -1.0e30

Q0, K0, V0, DQ, DK, DV, DZ, CA, CB = 0, 4, 5, 6, 8, 10, 12, 14, 16

C_COLS = {}
_at = 0
for _n, _w in (("ident", 128), ("ones", 128), ("bones", 128), ("rot", 128), ("istk", 64), ("amask", 256),
               ("mincT", 64), ("bd", 128), ("lev", 6 * 128), ("lev1c", 64), ("reset", 512),
               ("selb", 256), ("selg", 256), ("invf", 1), ("rotm", 1), ("nrotm", 1),
               ("eps", 1), ("eps64", 1), ("rank", 8)):
    C_COLS[_n] = (_at, _at + _w)
    _at += _w
N_CONST = _at

P_COLS = {}
_at = 0
for _n, _w in (("adab", 96), ("ng", 4 * DC), ("fg", DC), ("c", DC), ("wba", DEPTH * DC * 8), ("dtb", DEPTH),
               ("alog", DEPTH), ("sink", DEPTH * 8), ("dconv", DEPTH * 6 * 4), ("dng", DEPTH),
               ("cconv", DEPTH * 2 * CV_K), ("cb", DEPTH * 2), ("lng", DEPTH * 2), ("lnb", DEPTH * 2),
               ("rw", DC * NE), ("rb", NE)):
    P_COLS[_n] = (_at, _at + _w)
    _at += _w
N_PAR = _at

T_IN = [0, 70 + 16]
T_OUT = [18, 70 + 16 + 18]
T_GU0 = 26
T_DN0 = 70
T_MOE = 70 + 16 + 26
T_END = T_MOE + NE * 24
KD = FC // 2
U_IN = [1, 1 + 9 + 4 + 22 + 4]
U_OUT = [1 + 9, U_IN[1] + 9]
U_GU0 = U_OUT[0] + 4
U_DN0 = U_GU0 + 22
U_MOE = U_OUT[1] + 4
X_USES = [1, U_GU0, U_IN[1], U_MOE, U_MOE + NE * 12]


def constants():
    c = np.zeros((P, N_CONST), np.float32)

    def put(name, a):
        lo, hi = C_COLS[name]
        c[:a.shape[0], lo:hi] = a.reshape(a.shape[0], hi - lo)

    p = np.arange(P)
    j64 = np.arange(64)
    put("ident", np.eye(P))
    put("ones", np.ones((P, P)))
    same = (p[:, None] // 64 == p[None, :] // 64)
    put("bones", same * 1.0)
    rot = np.zeros((P, P))
    for b in (0, 64):
        for d in range(ROT // 2):
            rot[b + d + ROT // 2, b + d] = -1.0
            rot[b + d, b + d + ROT // 2] = 1.0
    put("rot", rot)
    put("istk", (p[:, None] % 64 == j64[None, :]) * 1.0)
    diff = p[:, None] + P - np.arange(2 * P)[None, :]
    put("amask", np.where((diff >= 0) & (diff < P), 0.0, NEG))
    put("mincT", np.where(j64[None, :] >= p[:, None] % 64, 0.0, NEG))
    put("bd", same * 1.0)
    lev = np.zeros((P, 6, P))
    for n in range(6):
        s = 1 << n
        row, col = p[None, :] % 64, p[:, None] % 64
        lev[:, n] = same & (row // (2 * s) == col // (2 * s)) & (row // s % 2 == 1) & (col // s % 2 == 0)
    put("lev", lev)
    put("lev1c", ((j64[None, :] // 2 == p[:, None] % 64 // 2) & (j64[None, :] % 2 == 1) & (p[:, None] % 2 == 0)) * 1.0)
    put("reset", np.tile((np.arange(S) % 64 != 0) * 1.0, (P, 1)))
    selb, selg = np.zeros((8, 2, P)), np.zeros((8, 2, P))
    for hp in range(2):
        for par in range(2):
            selb[hp * 2 + par, hp, par * 64:par * 64 + 64] = 1.0
            selg[4 + hp * 2 + par, hp, par * 64:par * 64 + 64] = 1.0
    put("selb", selb)
    put("selg", selg)
    inv = np.float32(500000.0) ** (-np.arange(0, ROT, 2, dtype=np.float32) / np.float32(ROT))
    d = p % 64
    put("invf", np.where(d < ROT, inv[d % (ROT // 2)], 0.0)[:, None])
    put("rotm", (d < ROT)[:, None] * 1.0)
    put("nrotm", (d >= ROT)[:, None] * 1.0)
    put("eps", np.full((P, 1), EPS))
    put("eps64", np.full((P, 1), 64 * EPS))
    put("rank", np.tile(8.0 - np.arange(8), (P, 1)))
    return c



def trunk(nc, xT, consts, params, pos, ada, w8, w11, outT):
    ctx = ExitStack()
    with ctx:
        def sb(name, shape, dt=F32, stack=ctx):
            return stack.enter_context(nc.sbuf_tensor(name, [P] + shape, dt))

        sems = {}

        def sem(name):
            if name not in sems:
                sems[name] = ctx.enter_context(nc.semaphore(name))
            return sems[name]

        cst = sb("cst", [N_CONST])
        par = sb("par", [N_PAR])
        x = sb("x", [DC, S])
        hhi = sb("hhi", [DC, S], F32R)
        hlo = sb("hlo", [DC, S], F32R)
        raw = sb("raw", [2, KD * P])
        whi = sb("whi", [2, KD * P], F32R)
        wlo = sb("wlo", [2, KD * P], F32R)
        mod = sb("mod", [96])
        sclg = sb("sclg", [4, DC])
        small = sb("small", [256])
        cosb = sb("cosb", [S])
        sinb = sb("sinb", [S])
        rstd = sb("rstd", [S])
        with ExitStack() as room:
            scr = sb("scr", [17 * 1024], stack=room)
            proj = sb("proj", [N_IN_TILES, S], stack=room)
        with ExitStack() as room:
            adar = sb("adar", [4, DC * 256], stack=room)
            posi = sb("posi", [S], I32, stack=room)
            ang = sb("ang", [4, S], stack=room)
            cact = sb("cact", [2 * DC], stack=room)
        with ExitStack() as room:
            ghi = sb("ghi", [FC, S], F32R, stack=room)
            glo = sb("glo", [FC, S], F32R, stack=room)
            sg = sb("sg", [S], stack=room)
            gt = sb("gt", [S], stack=room)
        with ExitStack() as room:
            sb("experts_hidden", [FE, S], stack=room)
            comb = sb("comb", [NE, S], stack=room)
            combt = sb("combt", [S], stack=room)
            combm = sb("combm", [S], stack=room)
            logit = sb("logit", [4 * NE * 8], stack=room)
        h = scr[:, 0:DC * S].rearrange("p (c s) -> p c s", c=DC)
        ps = ctx.enter_context(nc.psum_tensor("ps", [P, 8, 512], F32))

        def C(name, rows=P):
            lo, hi = C_COLS[name]
            return cst[0:rows, lo:hi]

        def PR(name, n=0, w=1, rows=P):
            lo, _ = P_COLS[name]
            return par[0:rows, lo + n:lo + n + w]

        def unit(n, w=1):
            return scr[:, n * 1024:(n + w) * 1024]

        def cmp(ap):
            return ap.rearrange("p (u j) -> p u j", u=NU)

        def bdv(ap):
            return ap.rearrange("p (u a j) -> p u a j", u=NU, a=2)

        def lhs(ap, u):
            return ap[:, u * P:(u + 1) * P]

        def two(b):
            return ps[:, b:b + 2, :].rearrange("p b (u j) -> p (b u) j", j=64)

        def over2(ap):
            return ap.unsqueeze(2).broadcast_to([P, NU, 2, 64])

        def mask4(m):
            return m.rearrange("p (a j) -> p a j", a=2).unsqueeze(1).broadcast_to([P, NU, 2, 64])

        def col(ap16):
            return ap16.unsqueeze(2).broadcast_to([P, NU, 64])

        QA, KA, VA, GCJ, BJ, ET, LT, AT, VB = (unit(n) for n in (0, 1, 2, 3, 4, 5, 6, 7, 8))
        KBD, VBD, KBG, KG = unit(9, 2), unit(11, 2), unit(13, 2), unit(15, 2)
        TT, TC = unit(3), unit(4)
        MT, TTBD, XBD = unit(9, 2), unit(11, 2), unit(1, 2)
        UC, WBD = unit(5), unit(13, 2)
        ST, STBD = unit(3)[:, 0:128], unit(3)[:, 256:512]
        VN, VNBD = unit(4)[:, 0:128], unit(4)[:, 256:512]
        gcI, bI, egl, t16, sI, kgI = (small[:, n * 16:n * 16 + 16] for n in range(6))
        mx, negm, esk, den, rden, rsum = (small[:, 96 + n * 8:104 + n * 8] for n in range(6))
        SM = unit(0, 2).rearrange("p (h k) -> p h k", h=8)
        EX = unit(2, 2).rearrange("p (h k) -> p h k", h=8)
        PT = unit(4).rearrange("p (c k q) -> p c k q", c=4, k=2)
        VTOK = unit(5)[:, 0:512].rearrange("p (n d) -> p n d", n=4)
        ROTT = unit(6, 3)[:, 0:5 * S].rearrange("p (c s) -> p c s", c=5)
        BA = unit(14)[0:8, 0:512]
        BROW = unit(14)[0:8, 512:1024]
        GROW = unit(15)[0:8, 0:512]
        GTMP = unit(15)[0:8, 512:1024]

        block = ctx.enter_context(nc.Block())

        @block.sync
        def _(sp):
            sp.dma_start(cst[:], consts).then_inc(sem("inputs_in"), 16)
            sp.dma_start(par[:], params).then_inc(sem("inputs_in"), 16)
            sp.dma_start(x[:], xT.rearrange("(c p) s -> p c s", p=P)).then_inc(sem("inputs_in"), 16)
            sp.dma_start(posi[:], pos.partition_broadcast(P)).then_inc(sem("inputs_in"), 16)

            def load_ada(i, j, first=False):
                if not first:
                    sp.wait_ge(sem("ada_used"), 4 * i + j - 3)
                sp.dma_start(adar[:, j, :], ada[bass.ds(4 * i + j, 1), :, :].rearrange("a p n -> p (a n)"))\
                    .then_inc(sem(f"ada_in{j}"), 16)

            for j in range(4):
                load_ada(0, j, True)
            with sp.Fori(1, 12) as i:
                for j in range(4):
                    load_ada(i, j)

            def load_tile(src, n, slot, g, width):
                sp.wait_ge(sem("lo_ready"), g - 1)
                sp.dma_start(raw[:, slot, 0:width], src[bass.ds(n, 1), :, :].rearrange("a p n -> p (a n)"))\
                    .then_inc(sem(f"tile_in{slot}"), 16)

            for j in range(2):
                sp.dma_start(raw[:, j, 0:DC * P], w8[j, :, :]).then_inc(sem(f"tile_in{j}"), 16)
            with sp.Fori(1, T_DN0 // 2) as i:
                for j in range(2):
                    load_tile(w8, 2 * i + j, j, 2 * i + j, DC * P)
            with sp.Fori(0, 8) as i:
                for j in range(2):
                    load_tile(w11, 2 * i + j, j, 2 * i + j + T_DN0, KD * P)
            with sp.Fori(0, (T_END + 2 - T_DN0 - 16) // 2) as i:
                for j in range(2):
                    load_tile(w8, 2 * i + j + T_DN0, j, 2 * i + j + T_DN0 + 16, DC * P)
            sp.wait_ge(sem("out_ready"), DC)
            sp.dma_start(outT.rearrange("(c p) s -> p c s", p=P), h).then_inc(sem("stored"), 16)
            sp.wait_ge(sem("stored"), 16)

        @block.gpsimd
        def _(pool):
            for name in ("bank_free0", "bank_free1", "glo_ready"):
                pool.sem_inc(sem(name), 1)

        @block.tensor
        def _(pe):
            pe.wait_ge(sem("inputs_in"), 64)
            pe.wait_ge(sem("cact_ready"), 1)

            def ada_group(i, j):
                for m in range(2):
                    for k in range(DC):
                        ins = pe.matmul(ps[:, 7, bass.ds(8 * i + 2 * j + m, 1)],
                                        adar[:, j, k * 256 + m * P:k * 256 + m * P + P],
                                        cact[:, k:k + 1], start=(k == 0), stop=(k == DC - 1))
                ins.then_inc(sem("ada_used"), 1)

            with pe.Fori(0, 12) as i:
                for j in range(4):
                    pe.wait_ge(sem(f"ada_in{j}"), 16 * i + 16)
                    ada_group(i, j)

            def squares(s):
                pe.wait_ge(sem("sq_ready"), s + 1)
                for k in range(DC):
                    ins = pe.matmul(ps[:, 2, :], C("ones"), h[:, k, :], start=(k == 0), stop=(k == DC - 1))
                ins.then_inc(sem("ssum_ready"), 1)

            def tile(g, slot, b, rhs_hi, rhs_lo, k0, kn, start, stop):
                pe.wait_ge(sem("lo_ready"), g + 1)
                n = 0
                for k in range(kn):
                    w_hi = whi[:, slot, k * P:(k + 1) * P]
                    w_lo = wlo[:, slot, k * P:(k + 1) * P]
                    for a, r in ((w_hi, rhs_hi), (w_hi, rhs_lo), (w_lo, rhs_hi)):
                        ins = pe.matmul(ps[:, b, :], a, r[:, k0 + k, :], start=(start and n == 0),
                                        stop=(stop and n == 3 * kn - 1))
                        n += 1
                ins.then_inc(sem("tile_done"), 1)

            def pairs(iters, g0, u0, rhs_hi, rhs_lo, base=0, ubase=0, hidden=None):
                with pe.Fori(0, iters) as i:
                    for j in range(2):
                        if hidden is not None and j == 0:
                            pe.wait_ge(sem("glo_ready"), hidden)
                        pe.wait_ge(sem(f"bank_free{j}"), u0 + ubase + i)
                        tile(g0 + base + 2 * i + j, j, j, rhs_hi, rhs_lo, 0, DC, True, True)

            def h_ready(s):
                pe.wait_ge(sem("h_ready"), 8 * s + 8)

            for layer in range(DEPTH):
                v = layer + 1
                squares(2 * layer)
                h_ready(2 * layer)
                for k in range(DC):
                    ins = pe.matmul(ps[0:8, 3, :], PR("wba", (layer * DC + k) * 8, 8), h[:, k, :],
                                    start=(k == 0), stop=(k == DC - 1))
                ins.then_inc(sem("ba_done"), 1)
                pairs(9, T_IN[layer], U_IN[layer], hhi, hlo)
                for j in range(2):
                    pe.wait_ge(sem(f"bank_free{j}"), U_IN[layer] + 9)
                pe.wait_ge(sem("ba_copied"), v)
                for n in range(5):
                    ins = pe.matmul(ps[:, 2 + n, :], C("rot"), proj[:, n, :], start=True, stop=True)
                ins.then_inc(sem("rot_done"), 1)
                for n in range(4):
                    ins = pe.transpose(ps[:, 7, n * P:(n + 1) * P], proj[:, V0, n * P:(n + 1) * P], C("ident"))
                ins.then_inc(sem("vt_done"), 1)
                pe.wait_ge(sem("rope_done"), v)
                pe.wait_ge(sem("vtok_ready"), v)
                for n in range(4):
                    q = slice(n * P, (n + 1) * P)
                    lo = P if n == 0 else 0
                    if n:
                        pe.wait_ge(sem("sm_ready"), 4 * layer + n)
                    for a in range(2):
                        r = slice(64 * a, 64 * a + 64)
                        for c in range(4):
                            ins = pe.matmul(ps[:, 2 * a + c // 2, (c % 2) * 256 + lo:(c % 2) * 256 + 256],
                                            proj[r, Q0 + c, q], proj[r, K0, (n - 1) * P + lo:(n + 1) * P],
                                            start=True, stop=True)
                    ins.then_inc(sem("scores_done"), 1)
                    pe.wait_ge(sem("probs_ready"), 4 * layer + n + 1)
                    for a in range(2):
                        m = 2 * (4 * layer + n) + a
                        if m:
                            pe.wait_ge(sem("pt_ready"), m)
                        for c in range(4):
                            for kb in range(lo // P, 2):
                                ins = pe.transpose(ps[:, 4 + c // 2, (c % 2) * 256 + kb * P:(c % 2) * 256 + kb * P + P],
                                                   EX[:, 4 * a + c, kb * P:(kb + 1) * P], C("ident"))
                        ins.then_inc(sem("pt_done"), 1)
                        pe.wait_ge(sem("pt_ready"), m + 1)
                        if a == 0 and 4 * layer + n:
                            pe.wait_ge(sem("ya_ready"), 4 * layer + n)
                        for c in range(4):
                            for kb in range(lo // P, 2):
                                ins = pe.matmul(ps[64 * a:64 * a + 64, 6, c * P:(c + 1) * P],
                                                VTOK[:, n - 1 + kb, 64 * a:64 * a + 64], PT[:, c, kb, :],
                                                start=(kb == lo // P), stop=(kb == 1))
                        ins.then_inc(sem("pv_done"), 1)
                pe.wait_ge(sem("dn_sq_ready"), v)
                pe.wait_ge(sem("ya_ready"), 4 * v)
                for n in range(4):
                    ins = pe.matmul(ps[:, 2 + n, :], C("bones"), unit(9, 2)[:, n * S:(n + 1) * S], start=True, stop=True)
                ins.then_inc(sem("dn_ss_done"), 1)
                pe.wait_ge(sem("beta_rows"), v)
                pe.wait_ge(sem("gate_rows"), v)
                for hp in range(2):
                    pe.matmul(ps[:, 6 + hp, :], C("selb", 8)[:, hp * P:(hp + 1) * P], BROW, start=True, stop=True)
                for hp in range(2):
                    ins = pe.matmul(ps[:, hp, :], C("selg", 8)[:, hp * P:(hp + 1) * P], GROW, start=True, stop=True)
                ins.then_inc(sem("rows_spread"), 1)
                pe.wait_ge(sem("kv_bd_ready"), 2 * v)
                pe.wait_ge(sem("bj_ready"), v)
                pe.wait_ge(sem("gcj_ready"), 2 * v)
                for u in range(NU):
                    o = slice((u % 8) * 64, (u % 8) * 64 + 64)
                    c = slice(u * 64, u * 64 + 64)
                    pe.matmul(ps[:, u // 8, o], lhs(KBD, u), KA[:, c], start=True, stop=True)
                    pe.matmul(ps[:, 2 + u // 8, o], lhs(KBD, u), QA[:, c], start=True, stop=True)
                    pe.matmul(ps[:, 4 + u // 8, o], lhs(KBD, u), C("istk"), start=True, stop=True)
                    ins = pe.matmul(ps[:, 6 + u // 8, o], lhs(VBD, u), C("istk"), start=True, stop=True)
                ins.then_inc(sem("gram_done"), 1)
                for lv in range(1, 6):
                    m = 5 * layer + lv - 1
                    pe.wait_ge(sem("tt_ready"), 5 * layer + lv)
                    for u in range(NU):
                        ins = pe.matmul(ps[:, u // 8, (u % 8) * 64:(u % 8) * 64 + 64], lhs(TTBD, u), C("istk"),
                                        start=True, stop=True)
                    ins.then_inc(sem("t_done"), 1)
                    pe.wait_ge(sem("tc_ready"), m + 1)
                    pe.wait_ge(sem("mt_ready"), m + 1)
                    for u in range(NU):
                        ins = pe.matmul(ps[:, 2 + u // 8, (u % 8) * 64:(u % 8) * 64 + 64], lhs(MT, u),
                                        TC[:, u * 64:u * 64 + 64], start=True, stop=True)
                    ins.then_inc(sem("x_done"), 1)
                    pe.wait_ge(sem("xbd_ready"), m + 1)
                    for u in range(NU):
                        ins = pe.matmul(ps[:, 4 + u // 8, (u % 8) * 64:(u % 8) * 64 + 64], lhs(XBD, u),
                                        TT[:, u * 64:u * 64 + 64], start=True, stop=True)
                    ins.then_inc(sem("yt_done"), 1)
                pe.wait_ge(sem("tt_final"), v)
                for u in range(NU):
                    o = slice((u % 8) * 64, (u % 8) * 64 + 64)
                    c = slice(u * 64, u * 64 + 64)
                    pe.matmul(ps[:, u // 8, o], lhs(TTBD, u), VB[:, c], start=True, stop=True)
                    ins = pe.matmul(ps[:, 2 + u // 8, o], lhs(KBG, u), TT[:, c], start=True, stop=True)
                ins.then_inc(sem("uw_done"), 1)
                for n in range(NCH):
                    m = NCH * layer + n
                    pe.wait_ge(sem("state_ready"), (NCH + 1) * layer + n + 1)
                    for hp in range(2):
                        ins = pe.matmul(ps[:, 4, hp * 64:hp * 64 + 64], lhs(WBD, hp * 8 + n), ST[:, hp * 64:hp * 64 + 64],
                                        start=True, stop=True)
                    ins.then_inc(sem("ws_done"), 1)
                    pe.wait_ge(sem("vnew_ready"), m + 1)
                    for hp in range(2):
                        u = hp * 8 + n
                        ins = pe.matmul(ps[:, 5, hp * 64:hp * 64 + 64], lhs(KG, u), VN[:, hp * 64:hp * 64 + 64],
                                        start=True, stop=True)
                    ins.then_inc(sem("kv_done"), 1)
                    for hp in range(2):
                        u = hp * 8 + n
                        pe.matmul(ps[:, 6 + hp, n * 64:n * 64 + 64], STBD[:, hp * P:(hp + 1) * P], QA[:, u * 64:u * 64 + 64],
                                  start=True, stop=False)
                        ins = pe.matmul(ps[:, 6 + hp, n * 64:n * 64 + 64], VNBD[:, hp * P:(hp + 1) * P],
                                        AT[:, u * 64:u * 64 + 64], start=False, stop=True)
                    ins.then_inc(sem("o_done"), 1)
                pe.wait_ge(sem("osq_ready"), v)
                for hp in range(2):
                    ins = pe.matmul(ps[:, hp, :], C("bones"), unit(9)[:, hp * S:(hp + 1) * S], start=True, stop=True)
                ins.then_inc(sem("oss_done"), 1)
                pe.wait_ge(sem("cv_ready"), v)
                for n in range(2):
                    ins = pe.matmul(ps[:, 2, :], C("ones"), proj[:, 6 + n, :], start=(n == 0), stop=(n == 1))
                ins.then_inc(sem("cmean_done"), 1)
                pe.wait_ge(sem("csq_ready"), v)
                for n in range(2):
                    ins = pe.matmul(ps[:, 3, :], C("ones"), proj[:, CB + n, :], start=(n == 0), stop=(n == 1))
                ins.then_inc(sem("cvar_done"), 1)
                pe.wait_ge(sem("ylo_ready"), v)
                pairs(4, T_OUT[layer], U_OUT[layer], hhi, hlo)
                squares(2 * layer + 1)
                h_ready(2 * layer + 1)
                if layer == 0:
                    pairs(FC, T_GU0, U_GU0, hhi, hlo)
                    pe.wait_ge(sem("glo_ready"), 1 + FC)
                    with pe.Fori(0, 4) as i:
                        for j in range(2):
                            pe.wait_ge(sem(f"bank_free{j}"), U_DN0 + i)
                            for half in range(2):
                                tile(T_DN0 + 4 * i + 2 * j + half, half, j, ghi, glo, half * KD, KD,
                                     half == 0, half == 1)
                else:
                    for t in range(4):
                        for k in range(DC):
                            ins = pe.matmul(ps[:, 3, t * NE:(t + 1) * NE], h[:, k, t * P:(t + 1) * P],
                                            PR("rw", k * NE, NE), start=(k == 0), stop=(k == DC - 1))
                    ins.then_inc(sem("logits_done"), 1)
                    pe.wait_ge(sem("combine_ready"), 1)
                    for t in range(4):
                        ins = pe.transpose(ps[0:NE, 4, t * P:(t + 1) * P], logit[:, 64 + t * NE:64 + (t + 1) * NE], C("ident"))
                    ins.then_inc(sem("combt_done"), 1)
                    for e in range(NE):
                        pe.wait_ge(sem("combm_ready"), e + 1)
                        pe.matmul(ps[:, 5, :], C("ones", NE), combm[0:NE, :], start=True, stop=True)\
                            .then_inc(sem("comb_done"), 1)
                    with pe.Fori(0, NE) as e:
                        pairs(FE, T_MOE, U_MOE, hhi, hlo, 24 * e, 12 * e)
                        pairs(4, T_MOE + 16, U_MOE + 8, ghi, glo, 24 * e, 12 * e, 1 + FC + FE + FE * e)
            squares(4)

        @block.scalar
        def _(act):
            count = {}

            def mark(ins, name, n=1):
                count[name] = count.get(name, 0) + n
                ins.then_inc(sem(name), 1)
                act.wait_ge(sem(name), count[name])

            def split(slot, g, use, width=DC * P):
                act.wait_ge(sem(f"tile_in{slot}"), use)
                if not (isinstance(g, int) and g < 2):
                    act.wait_ge(sem("tile_done"), g - 1)
                act.activation(whi[:, slot, 0:width], raw[:, slot, 0:width], ACT.Copy).then_inc(sem("hi_ready"), 1)

            def use_of(g_half):
                return 16 * g_half + 16

            def norm(s):
                if s:
                    for j in range(2):
                        act.wait_ge(sem(f"bank_free{j}"), X_USES[s])
                act.activation(h, x[:], ACT.Square).then_inc(sem("sq_ready"), 1)
                act.wait_ge(sem("ssum_ready"), s + 1)
                act.activation(rstd[:], ps[:, 2, :], ACT.Sqrt, scale=1.0 / D, bias=C("eps")).then_inc(sem("rms_ready"), 1)
                if s == 4:
                    return
                for k in range(DC):
                    act.wait_ge(sem("hn_ready"), 8 * s + k + 1)
                    mark(act.activation(h[:, k, :], h[:, k, :], ACT.Identity, scale=sclg[:, s, k:k + 1],
                                        bias=mod[:, s * 24 + k:s * 24 + k + 1]), "hs_ready")
                    act.activation(hhi[:, k, :], h[:, k, :], ACT.Copy).then_inc(sem("hhi_ready"), 1)

            act.wait_ge(sem("inputs_in"), 64)
            act.activation(cact[:, 0:DC], PR("c", 0, DC), ACT.Silu).then_inc(sem("cact_ready"), 1)
            act.wait_ge(sem("ang_ready"), 2)
            act.activation(sinb[:], ang[:, 2, :], ACT.Sin).then_inc(sem("sincos"), 1)
            act.activation(cosb[:], ang[:, 3, :], ACT.Sin).then_inc(sem("sincos"), 1)
            for g in range(2):
                split(g, g, 16)
            act.wait_ge(sem("mod_ready"), 2)

            for layer in range(DEPTH):
                v = layer + 1
                norm(2 * layer)
                g0 = T_IN[layer]
                with act.Fori(0, 9) as i:
                    for j in range(2):
                        split(j, g0 + 2 * i + j + 2, 16 * i + 8 * g0 + 32)
                        act.wait_ge(sem("tile_done"), g0 + 2 * i + j + 1)
                        act.activation(proj[:, bass.ds(2 * i + j, 1), :], ps[:, j:j + 1, :], ACT.Copy)\
                            .then_inc(sem(f"bank_free{j}"), 1)
                for j in range(2):
                    act.wait_ge(sem(f"bank_free{j}"), U_IN[layer] + 9)
                for n in range(4):
                    lo = P if n == 0 else 0
                    act.wait_ge(sem("mx_ready"), 4 * layer + n + 1)
                    act.wait_ge(sem("sm_ready"), 4 * layer + n + 1)
                    if 4 * layer + n:
                        act.wait_ge(sem("pt_done"), 2 * (4 * layer + n))
                    for hd in range(8):
                        ins = act.activation(EX[:, hd, lo:256], SM[:, hd, lo:256], ACT.Exp,
                                             bias=negm[:, hd:hd + 1], accum_out=rsum[:, hd:hd + 1])
                    ins.then_inc(sem("exp_ready"), 1)
                    act.wait_ge(sem("esk_in"), 4 * layer + n + 1)
                    act.activation(esk, den, ACT.Exp).then_inc(sem("esk_ready"), 1)
                    for a in range(2):
                        act.wait_ge(sem("pt_done"), 2 * (4 * layer + n) + a + 1)
                        if a or n or layer:
                            act.wait_ge(sem("pv_done"), 2 * (4 * layer + n) + a)
                        act.activation(PT[:, :, lo // P:2, :],
                                       ps[:, 4:6, :].rearrange("p b (c k q) -> p (b c) k q", c=2, k=2)[:, :, lo // P:2, :],
                                       ACT.Copy).then_inc(sem("pt_ready"), 1)
                act.wait_ge(sem("dconv_done"), v)
                mark(act.activation(unit(0, 3), unit(0, 3), ACT.Silu), "dsilu_ready")
                mark(act.activation(proj[:, DZ:DZ + 2, :], proj[:, DZ:DZ + 2, :], ACT.Silu), "zsilu_ready")
                act.activation(proj[:, CB:CB + 2, :], proj[:, CB:CB + 2, :], ACT.Sigmoid).then_inc(sem("csig_ready"), 1)
                act.activation(unit(9, 2), unit(0, 2), ACT.Square).then_inc(sem("dn_sq_ready"), 1)
                act.wait_ge(sem("rows_in"), v)
                mark(act.activation(BROW, BA, ACT.Sigmoid), "beta_rows")
                act.wait_ge(sem("dn_ss_done"), v)
                act.activation(unit(11, 2)[:, 0:1024], ps[:, 2:4, :].rearrange("p b n -> p (b n)"), ACT.Sqrt,
                               scale=64.0, bias=C("eps64"))
                act.activation(unit(11, 2)[:, 1024:2048], ps[:, 4:6, :].rearrange("p b n -> p (b n)"), ACT.Sqrt,
                               bias=C("eps")).then_inc(sem("dn_norm_ready"), 1)
                mark(act.activation(GTMP, GROW, ACT.Abs), "g_abs")
                mark(act.activation(GTMP, GTMP, ACT.Exp, scale=-1.0), "g_exp")
                act.activation(GTMP, GTMP, ACT.Ln, bias=1.0).then_inc(sem("g_ln"), 1)
                act.activation(small[0:8, 200:201], PR("alog", layer, 1, 8), ACT.Exp).then_inc(sem("g_ln"), 1)
                act.wait_ge(sem("rows_spread"), v)
                act.activation(BJ, ps[:, 6:8, :].rearrange("p b n -> p (b n)"), ACT.Copy).then_inc(sem("bj_ready"), 1)
                act.wait_ge(sem("dift_ready"), v)
                act.activation(ET, ET, ACT.Exp).then_inc(sem("et_ready"), 1)
                act.wait_ge(sem("gci_ready"), v)
                act.activation(t16, gcI, ACT.Exp).then_inc(sem("egi_ready"), 1)
                act.activation(egl, cmp(GCJ)[:, :, 63], ACT.Exp).then_inc(sem("egi_ready"), 1)
                act.activation(kgI, kgI, ACT.Exp).then_inc(sem("egi_ready"), 1)
                act.wait_ge(sem("gram_done"), v)
                act.wait_ge(sem("gram_read"), v)
                act.activation(KA, GCJ, ACT.Exp).then_inc(sem("egj_ready"), 1)
                for lv in range(1, 6):
                    act.wait_ge(sem("t_done"), 5 * layer + lv)
                    act.wait_ge(sem("tt_ready"), 5 * layer + lv)
                    act.activation(TC, ps[:, 0:2, :].rearrange("p b n -> p (b n)"), ACT.Copy).then_inc(sem("tc_ready"), 1)
                act.wait_ge(sem("uw_done"), v)
                act.activation(UC, ps[:, 0:2, :].rearrange("p b n -> p (b n)"), ACT.Copy).then_inc(sem("uc_ready"), 1)
                act.wait_ge(sem("o_done"), NCH * v)
                act.activation(unit(9), ps[:, 6:8, :].rearrange("p b n -> p (b n)"), ACT.Square).then_inc(sem("osq_ready"), 1)
                act.wait_ge(sem("oss_done"), v)
                act.activation(unit(10), ps[:, 0:2, :].rearrange("p b n -> p (b n)"), ACT.Sqrt, scale=1.0 / 64,
                               bias=C("eps")).then_inc(sem("orms_ready"), 1)
                act.wait_ge(sem("cxc_ready"), v)
                act.activation(proj[:, CB:CB + 2, :], proj[:, 6:8, :], ACT.Square).then_inc(sem("csq_ready"), 1)
                act.wait_ge(sem("cvar_done"), v)
                act.activation(rstd[:], ps[:, 3, :], ACT.Sqrt, scale=1.0 / 256, bias=C("eps")).then_inc(sem("crms_ready"), 1)
                act.wait_ge(sem("cn_ready"), v)
                for n in range(2):
                    mark(act.activation(proj[:, 6 + n, :], proj[:, 6 + n, :], ACT.Silu,
                                        scale=PR("lng", layer * 2 + n), bias=PR("lnb", layer * 2 + n)), "cy_ready")
                act.wait_ge(sem("yd_ready"), v)
                act.activation(hhi[:], proj[:, 0:8, :], ACT.Copy).then_inc(sem("yhi_ready"), 1)
                g0 = T_OUT[layer]
                with act.Fori(0, 4) as i:
                    for j in range(2):
                        split(j, g0 + 2 * i + j + 2, 16 * i + 8 * g0 + 32)
                norm(2 * layer + 1)

                def gate_up(g0, k0, u0, off=0, uoff=0):
                    def step(i, j, width):
                        split(j, g0 + off + 2 * i + j + 2, 16 * i + 8 * (g0 + off) + 32, width)

                    def one(i, width):
                        step(i, 0, width)
                        act.wait_ge(sem("tile_done"), g0 + off + 2 * i + 1)
                        act.wait_ge(sem("bank_free1"), u0 + uoff + i)
                        act.activation(sg[:], ps[:, 0, :], ACT.Silu).then_inc(sem("bank_free0"), 1)
                        step(i, 1, width)
                        if layer == 0:
                            act.wait_ge(sem("bank_free1"), u0 + uoff + i + 1)
                        else:
                            act.wait_ge(sem("gt_ready"), k0 - FC + i + 1)
                        act.activation(ghi[:, bass.ds(i, 1), :], gt[:].unsqueeze(1), ACT.Copy).then_inc(sem("ghi_ready"), 1)
                    return one

                if layer == 0:
                    one = gate_up(T_GU0, 0, U_GU0)
                    with act.Fori(0, FC - 1) as i:
                        one(i, DC * P)
                    with act.Fori(FC - 1, FC) as i:
                        one(i, KD * P)
                    with act.Fori(0, 7) as i:
                        for j in range(2):
                            split(j, T_DN0 + 2 * i + j + 2, 16 * i + 8 * T_DN0 + 32, KD * P)
                    for j in range(2):
                        split(j, T_DN0 + 16 + j, 16 * 7 + 8 * T_DN0 + 32)
                else:
                    act.wait_ge(sem("route_in"), 1)
                    act.activation(small[:, 212:216], small[:, 212:216], ACT.Exp).then_inc(sem("route_exp"), 1)
                    with act.Fori(0, NE) as e:
                        one = gate_up(T_MOE, FC + FE * e, U_MOE, 24 * e, 12 * e)
                        with act.Fori(0, FE) as i:
                            one(i, DC * P)
                        with act.Fori(0, 4) as i:
                            for j in range(2):
                                split(j, T_MOE + 16 + 24 * e + 2 * i + j + 2, 16 * i + 8 * (T_MOE + 16 + 24 * e) + 32)
            norm(4)

        @block.vector
        def _(dve):
            count = {}
            here = [0]

            def link(ins):
                here[0] += 1
                ins.then_inc(sem("dve_step"), 1)
                dve.wait_ge(sem("dve_step"), here[0])

            def mark(ins, name):
                count[name] = count.get(name, 0) + 1
                ins.then_inc(sem(name), 1)
                dve.wait_ge(sem(name), count[name])

            def tt(out, a, b, op=ALU.mult):
                return dve.tensor_tensor(out, a, b, op)

            def stt(out, a, s, b, op0=ALU.mult, op1=ALU.add):
                return dve.scalar_tensor_tensor(out=out, in0=a, scalar=s, in1=b, op0=op0, op1=op1)

            def split(slot, g, width=DC * P):
                dve.wait_ge(sem("hi_ready"), g + 1)
                dve.tensor_tensor(wlo[:, slot, 0:width], raw[:, slot, 0:width], whi[:, slot, 0:width].bitcast(F32),
                                  ALU.subtract).then_inc(sem("lo_ready"), 1)

            def norm(s):
                dve.wait_ge(sem("rms_ready"), s + 1)
                link(dve.reciprocal(rstd[:], rstd[:]))
                if s == 4:
                    for k in range(DC):
                        stt(h[:, k, :], x[:, k, :], PR("fg", k), rstd[:], ALU.mult, ALU.mult).then_inc(sem("out_ready"), 1)
                    return
                for k in range(DC):
                    tt(h[:, k, :], x[:, k, :], rstd[:]).then_inc(sem("hn_ready"), 1)
                for k in range(DC):
                    dve.wait_ge(sem("hhi_ready"), 8 * s + k + 1)
                    tt(hlo[:, k, :], h[:, k, :], hhi[:, k, :].bitcast(F32), ALU.subtract).then_inc(sem("h_ready"), 1)

            dve.wait_ge(sem("inputs_in"), 64)
            two_pi = 2 * np.pi
            c1 = 6.28125
            c2 = float(np.float32(np.round((two_pi - c1) * 2 ** 17) / 2 ** 17))
            c3 = float(np.float32(np.round((two_pi - c1 - c2) * 2 ** 26) / 2 ** 26))
            c4 = float(np.float32(two_pi - c1 - c2 - c3))
            magic = 12582912.0
            link(dve.tensor_copy(ang[:, 0, :], posi[:]))
            link(dve.tensor_scalar(ang[:, 0, :], ang[:, 0, :], C("invf"), None, ALU.mult))
            for n, shift in ((2, 0.0), (3, 0.25)):
                link(dve.tensor_scalar(ang[:, 1, :], ang[:, 0, :], float(1 / two_pi), shift, ALU.mult, ALU.add))
                link(dve.tensor_scalar(ang[:, 1, :], ang[:, 1, :], magic, None, ALU.add))
                link(dve.tensor_scalar(ang[:, 1, :], ang[:, 1, :], magic, None, ALU.subtract))
                prev = ang[:, 0, :]
                for cc in (c1, c2, c3, c4):
                    link(stt(ang[:, n, :], ang[:, 1, :], -cc, prev))
                    prev = ang[:, n, :]
                link(dve.tensor_scalar(ang[:, n, :], ang[:, n, :], float(two_pi * shift), float(np.float32(3.1415925)),
                                       ALU.add, ALU.min))
                dve.tensor_scalar(ang[:, n, :], ang[:, n, :], -float(np.float32(3.1415925)), None, ALU.max)\
                    .then_inc(sem("ang_ready"), 1)
            dve.wait_ge(sem("sincos"), 2)
            link(dve.tensor_scalar(cosb[:], cosb[:], C("rotm"), C("nrotm"), ALU.mult, ALU.add))
            link(dve.tensor_scalar(sinb[:], sinb[:], C("rotm"), None, ALU.mult))
            for g in range(2):
                split(g, g)
            dve.wait_ge(sem("ada_used"), 48)
            mark(tt(mod[:], ps[:, 7, 0:96], PR("adab", 0, 96), ALU.add), "mod_ready")
            mark(stt(sclg[:], mod[:].rearrange("p (s t k) -> p s t k", s=4, t=3)[:, :, 1, :], 1.0,
                     PR("ng", 0, 4 * DC).rearrange("p (s k) -> p s k", s=4), ALU.add, ALU.mult), "mod_ready")

            for layer in range(DEPTH):
                v = layer + 1
                norm(2 * layer)
                g0 = T_IN[layer]
                with dve.Fori(0, 9) as i:
                    for j in range(2):
                        split(j, g0 + 2 * i + j + 2)
                dve.wait_ge(sem("ba_done"), v)
                dve.tensor_copy(BA, ps[0:8, 3, :]).then_inc(sem("ba_copied"), 1)
                dve.wait_ge(sem("rot_done"), v)
                bc = lambda ap: ap.unsqueeze(1).broadcast_to([P, 5, S])
                link(tt(ROTT, ps[:, 2:7, :], bc(sinb[:])))
                link(tt(proj[:, 0:5, :], proj[:, 0:5, :], bc(cosb[:])))
                tt(proj[:, 0:5, :], proj[:, 0:5, :], ROTT, ALU.add).then_inc(sem("rope_done"), 1)
                dve.wait_ge(sem("vt_done"), v)
                dve.tensor_copy(VTOK, ps[:, 7, :].rearrange("p (n d) -> p n d", n=4)).then_inc(sem("vtok_ready"), 1)
                for n in range(4):
                    lo = P if n == 0 else 0
                    w = 256 - lo
                    dve.wait_ge(sem("scores_done"), 4 * layer + n + 1)
                    if 4 * layer + n:
                        dve.wait_ge(sem("exp_ready"), 4 * layer + n)
                    sv = ps[:, 0:4, :].rearrange("p b (c k) -> p (b c) k", c=2)[:, :, lo:256]
                    am = C("amask")[:, lo:256].unsqueeze(1).broadcast_to([P, 8, w])
                    mark(stt(SM[:, :, lo:256], sv, HD ** -0.5, am), "sm_ready")
                    link(dve.tensor_reduce(mx, SM[:, :, lo:256], AX.X, ALU.max))
                    link(tt(mx, mx, PR("sink", layer * 8, 8), ALU.max))
                    mark(dve.tensor_scalar(negm, mx, -1.0, None, ALU.mult), "mx_ready")
                    mark(tt(den, PR("sink", layer * 8, 8), mx, ALU.subtract), "esk_in")
                    dve.wait_ge(sem("exp_ready"), 4 * layer + n + 1)
                    dve.wait_ge(sem("esk_ready"), 4 * layer + n + 1)
                    link(tt(den, rsum, esk, ALU.add))
                    link(dve.reciprocal(rden, den))
                    tt(EX[:, :, lo:256], EX[:, :, lo:256], rden.unsqueeze(2).broadcast_to([P, 8, w]))\
                        .then_inc(sem("probs_ready"), 1)
                    dve.wait_ge(sem("pv_done"), 2 * (4 * layer + n) + 2)
                    dve.tensor_copy(proj[:, 0:4, n * P:(n + 1) * P], ps[:, 6, :].rearrange("p (c q) -> p c q", c=4))\
                        .then_inc(sem("ya_ready"), 1)
                for n in range(6):
                    o = unit(0, 3)[:, n * S:(n + 1) * S]
                    src = proj[:, DQ + n, :]
                    w = lambda k: PR("dconv", (layer * 6 + n) * 4 + k)
                    link(dve.tensor_scalar(o, src, w(3), None, ALU.mult))
                    for k in (2, 1, 0):
                        d = 3 - k
                        if (n, k) == (5, 0):
                            stt(o[:, d:], src[:, :S - d], w(k), o[:, d:]).then_inc(sem("dconv_done"), 1)
                        else:
                            link(stt(o[:, d:], src[:, :S - d], w(k), o[:, d:]))
                dve.wait_ge(sem("ba_copied"), v)
                mark(dve.tensor_scalar(GROW, BA, PR("dtb", layer, 1, 8), None, ALU.add), "rows_in")
                dve.wait_ge(sem("csig_ready"), v)
                link(tt(proj[:, CA:CA + 2, :], proj[:, CA:CA + 2, :], proj[:, CB:CB + 2, :]))
                dve.wait_ge(sem("g_ln"), 2 * v)
                link(dve.tensor_scalar(GROW, GROW, 0.0, None, ALU.max))
                link(tt(GROW, GROW, GTMP, ALU.add))
                mark(dve.tensor_scalar(small[0:8, 201:202], small[0:8, 200:201], -1.0, None, ALU.mult), "alog_neg")
                dve.tensor_scalar(GROW, GROW, small[0:8, 201:202], None, ALU.mult).then_inc(sem("gate_rows"), 1)
                dve.wait_ge(sem("dn_norm_ready"), v)
                link(dve.reciprocal(unit(11, 2), unit(11, 2)))
                link(tt(unit(0, 2), unit(0, 2), unit(11, 2)))
                mark(tt(bdv(KBD), over2(cmp(KA)), mask4(C("bd"))), "kv_bd_ready")
                mark(tt(bdv(VBD), over2(cmp(VA)), mask4(C("bd"))), "kv_bd_ready")
                dve.wait_ge(sem("rows_spread"), v)
                for hp in range(2):
                    mark(dve.tensor_tensor_scan(GCJ[:, hp * S:(hp + 1) * S], C("reset"), ps[:, hp, :], 0.0,
                                                ALU.mult, ALU.add), "gcj_ready")
                dve.wait_ge(sem("bj_ready"), v)
                istk = C("istk").unsqueeze(1).broadcast_to([P, NU, 64])
                link(tt(cmp(LT), cmp(GCJ), istk))
                mark(dve.tensor_reduce(gcI, cmp(LT), AX.X, ALU.add), "gci_tmp")
                link(tt(cmp(LT), cmp(BJ), istk))
                link(dve.tensor_reduce(bI, cmp(LT), AX.X, ALU.add))
                link(tt(cmp(ET), cmp(GCJ), col(gcI), ALU.subtract))
                mark(tt(cmp(ET), cmp(ET), C("mincT").unsqueeze(1).broadcast_to([P, NU, 64]), ALU.add), "dift_ready")
                mark(tt(kgI, cmp(GCJ)[:, :, 63], gcI, ALU.subtract), "gci_ready")
                dve.wait_ge(sem("egi_ready"), 3 * v)
                link(tt(sI, bI, t16))
                dve.wait_ge(sem("gram_done"), v)
                dve.wait_ge(sem("et_ready"), v)
                link(tt(cmp(LT), two(0), cmp(ET)))
                link(tt(LT, LT, BJ))
                link(tt(cmp(AT), two(2), cmp(ET)))
                link(tt(cmp(ET), two(4), col(sI)))
                link(tt(bdv(KBG), over2(cmp(ET)), mask4(C("bd"))))
                link(tt(cmp(ET), two(4), col(kgI)))
                link(tt(bdv(KG), over2(cmp(ET)), mask4(C("bd"))))
                mark(tt(cmp(VB), two(6), col(bI)), "gram_read")
                dve.wait_ge(sem("egj_ready"), v)
                link(tt(QA, QA, KA))
                lev = lambda n: C("lev")[:, n * P:(n + 1) * P]
                link(tt(bdv(TTBD), over2(cmp(LT)), mask4(lev(0))))
                link(tt(bdv(TTBD), mask4(C("ident")), bdv(TTBD), ALU.subtract))
                link(tt(cmp(TT), cmp(LT), C("lev1c").unsqueeze(1).broadcast_to([P, NU, 64])))
                mark(tt(cmp(TT), istk, cmp(TT), ALU.subtract), "tt_ready")
                for lv in range(1, 6):
                    m = 5 * layer + lv
                    mark(tt(bdv(MT), over2(cmp(LT)), mask4(lev(lv))), "mt_ready")
                    dve.wait_ge(sem("x_done"), m)
                    mark(tt(bdv(XBD), over2(two(2)), mask4(C("bd"))), "xbd_ready")
                    dve.wait_ge(sem("yt_done"), m)
                    link(tt(cmp(TT), cmp(TT), two(4), ALU.subtract))
                    mark(tt(bdv(TTBD), over2(cmp(TT)), mask4(C("bd"))), "tt_ready" if lv < 5 else "tt_final")
                dve.wait_ge(sem("uw_done"), v)
                link(tt(bdv(WBD), over2(two(2)), mask4(C("bd"))))
                dve.wait_ge(sem("uc_ready"), v)
                link(dve.memset(ST, 0.0))
                mark(dve.memset(STBD, 0.0), "state_ready")
                pr2 = lambda ap: ap.rearrange("p (a j) -> p a j", a=2)
                pr4 = lambda ap: ap.rearrange("p (u a j) -> p u a j", u=2, a=2)
                bd2 = C("bd").rearrange("p (a j) -> p a j", a=2).unsqueeze(1).broadcast_to([P, 2, 2, 64])
                uc3 = UC.rearrange("p (u n j) -> p u n j", u=2, n=NCH)
                for n in range(NCH):
                    m = NCH * layer + n
                    dve.wait_ge(sem("ws_done"), m + 1)
                    if m:
                        dve.wait_ge(sem("o_done"), m)
                    link(tt(pr2(VN), uc3[:, :, n, :], ps[:, 4, 0:128].rearrange("p (a j) -> p a j", a=2), ALU.subtract))
                    mark(tt(pr4(VNBD), pr2(VN).unsqueeze(2).broadcast_to([P, 2, 2, 64]), bd2), "vnew_ready")
                    dve.wait_ge(sem("kv_done"), m + 1)
                    dve.wait_ge(sem("o_done"), m + 1)
                    for hp in range(2):
                        o = ST[:, hp * 64:hp * 64 + 64]
                        link(stt(o, o, egl[:, hp * 8 + n:hp * 8 + n + 1], ps[:, 5, hp * 64:hp * 64 + 64]))
                    mark(tt(pr4(STBD), pr2(ST).unsqueeze(2).broadcast_to([P, 2, 2, 64]), bd2), "state_ready")
                dve.wait_ge(sem("orms_ready"), v)
                link(dve.reciprocal(unit(10), unit(10)))
                dve.wait_ge(sem("osq_ready"), v)
                yd = proj[:, 4:6, :]
                link(tt(yd, ps[:, 6:8, :], unit(10).rearrange("p (a s) -> p a s", a=2)))
                dve.wait_ge(sem("zsilu_ready"), v)
                mark(stt(yd, yd, PR("dng", layer), proj[:, DZ:DZ + 2, :], ALU.mult, ALU.mult), "yd_ready")
                for n in range(2):
                    o = proj[:, 6 + n, :]
                    src = proj[:, CA + n, :]
                    w = lambda k: PR("cconv", (layer * 2 + n) * CV_K + k)
                    link(dve.tensor_scalar(o, src, w(CV_K - 1), PR("cb", layer * 2 + n), ALU.mult, ALU.add))
                    for d in range(1, CV_K):
                        ins = stt(o[:, d:], src[:, :S - d], w(CV_K - 1 - d), o[:, d:])
                        if (n, d) == (1, CV_K - 1):
                            mark(ins, "cv_ready")
                        else:
                            link(ins)
                dve.wait_ge(sem("cmean_done"), v)
                cy = proj[:, 6:8, :]
                mark(stt(cy, ps[:, 2:3, :].broadcast_to([P, 2, S]), -1.0 / 256, cy), "cxc_ready")
                dve.wait_ge(sem("crms_ready"), v)
                link(dve.reciprocal(rstd[:], rstd[:]))
                mark(tt(cy, cy, rstd[:].unsqueeze(1).broadcast_to([P, 2, S])), "cn_ready")
                dve.wait_ge(sem("yhi_ready"), v)
                mark(tt(hlo[:], proj[:, 0:8, :], hhi[:].bitcast(F32), ALU.subtract), "ylo_ready")

                def residual(n, j, done, gate, uses):
                    dve.wait_ge(sem("tile_done"), done)
                    dve.wait_ge(sem(f"bank_free{j}"), uses)
                    stt(x[:, bass.ds(n, 1), :], ps[:, j:j + 1, :], mod[:, bass.ds(n + gate, 1)], x[:, bass.ds(n, 1), :])\
                        .then_inc(sem(f"bank_free{j}"), 1)

                g0 = T_OUT[layer]
                with dve.Fori(0, 4) as i:
                    for j in range(2):
                        split(j, g0 + 2 * i + j + 2)
                        residual(2 * i + j, j, g0 + 2 * i + j + 1, layer * 48 + 16, U_OUT[layer] + i)
                for j in range(2):
                    dve.wait_ge(sem(f"bank_free{j}"), X_USES[2 * layer + 1])
                norm(2 * layer + 1)

                def gate_up(i, g0, k0, u0, width, e=None):
                    for j in range(2):
                        split(j, g0 + 2 * i + j + 2, width)
                    dve.wait_ge(sem("tile_done"), g0 + 2 * i + 2)
                    dve.wait_ge(sem("bank_free0"), u0 + i + 1)
                    dve.wait_ge(sem("glo_ready"), k0 + i + 1)
                    if e is None:
                        tt(gt[:].unsqueeze(1), ps[:, 1:2, :], sg[:].unsqueeze(1)).then_inc(sem("bank_free1"), 1)
                    else:
                        tt(gt[:].unsqueeze(1), ps[:, 1:2, :], sg[:].unsqueeze(1)).then_inc(sem("bank_free1"), 1)
                        dve.wait_ge(sem("bank_free1"), u0 + i + 1)
                        tt(gt[:].unsqueeze(1), gt[:].unsqueeze(1), comb[:, bass.ds(e, 1), :]).then_inc(sem("gt_ready"), 1)
                    dve.wait_ge(sem("ghi_ready"), k0 + i + 1)
                    tt(glo[:, bass.ds(i, 1), :], gt[:].unsqueeze(1), ghi[:, bass.ds(i, 1), :].bitcast(F32), ALU.subtract)\
                        .then_inc(sem("glo_ready"), 1)

                if layer == 0:
                    with dve.Fori(0, FC - 1) as i:
                        gate_up(i, T_GU0, 0, U_GU0, DC * P)
                    with dve.Fori(FC - 1, FC) as i:
                        gate_up(i, T_GU0, 0, U_GU0, KD * P)

                    def down(i, widths):
                        for j in range(2):
                            for half in range(2):
                                split(half, T_DN0 + 4 * i + 2 * j + half + 2, widths[j])
                            residual(2 * i + j, j, T_DN0 + 4 * i + 2 * j + 2, 24 + 16, U_DN0 + i)

                    with dve.Fori(0, 3) as i:
                        down(i, (KD * P, KD * P))
                    with dve.Fori(3, 4) as i:
                        down(i, (KD * P, DC * P))
                    for j in range(2):
                        dve.wait_ge(sem(f"bank_free{j}"), X_USES[2])
                else:
                    def slot(n):
                        return logit[:, n * 32:(n + 1) * 32].rearrange("p (t e) -> p t e", t=4)

                    def four(n):
                        return small[:, 204 + 4 * n:208 + 4 * n]

                    def wide(ap):
                        return ap.unsqueeze(2).broadcast_to([P, 4, NE])

                    dve.wait_ge(sem("logits_done"), 1)
                    link(tt(slot(0), ps[:, 3, 0:32].rearrange("p (t e) -> p t e", t=4),
                            PR("rb", 0, NE).unsqueeze(1).broadcast_to([P, 4, NE]), ALU.add))
                    for n, (src, hot) in enumerate(((0, 3), (4, 5))):
                        link(dve.tensor_reduce(four(n), slot(src), AX.X, ALU.max))
                        link(tt(slot(1), slot(src), wide(four(n)), ALU.is_equal))
                        link(tt(slot(1), slot(1), C("rank").unsqueeze(1).broadcast_to([P, 4, NE])))
                        link(dve.tensor_reduce(four(3), slot(1), AX.X, ALU.max))
                        link(tt(slot(hot), slot(1), wide(four(3)), ALU.is_equal))
                        if n == 0:
                            link(stt(slot(4), slot(3), NEG, slot(0)))
                    mark(tt(four(2), four(1), four(0), ALU.subtract), "route_in")
                    dve.wait_ge(sem("route_exp"), 1)
                    link(dve.tensor_scalar(four(3), four(2), 1.0, None, ALU.add))
                    link(dve.reciprocal(four(3), four(3)))
                    link(tt(four(2), four(2), four(3)))
                    link(tt(slot(3), slot(3), wide(four(3))))
                    link(tt(slot(5), slot(5), wide(four(2))))
                    mark(tt(slot(2), slot(3), slot(5), ALU.add), "combine_ready")
                    dve.wait_ge(sem("combt_done"), 1)
                    link(dve.tensor_copy(combt[0:NE, :], ps[0:NE, 4, :]))
                    for e in range(NE):
                        mark(dve.tensor_scalar(combm[0:NE, :], combt[0:NE, :], C("ident", NE)[:, e:e + 1], None, ALU.mult),
                             "combm_ready")
                        dve.wait_ge(sem("comb_done"), e + 1)
                        link(dve.tensor_copy(comb[:, e, :], ps[:, 5, :]))
                    with dve.Fori(0, NE) as e:
                        with dve.Fori(0, FE) as i:
                            gate_up(i, T_MOE + 24 * e, FC + FE * e, U_MOE + 12 * e, DC * P, e)
                        with dve.Fori(0, 4) as i:
                            for j in range(2):
                                split(j, T_MOE + 16 + 24 * e + 2 * i + j + 2)
                                residual(2 * i + j, j, T_MOE + 16 + 24 * e + 2 * i + j + 1, 72 + 16,
                                         U_MOE + 8 + 12 * e + i)
                    for j in range(2):
                        dve.wait_ge(sem(f"bank_free{j}"), X_USES[4])
            norm(4)


def _chunks(a):
    return a.reshape((-1, P) + a.shape[1:]).swapaxes(0, 1)


def _tiles(w):
    k, n = w.shape
    return w.reshape(k // P, P, n // P, P).transpose(2, 1, 0, 3).reshape(n // P, P, k)


def kernel(**inputs):
    import concourse.bacc as _bacc
    from concourse.bass_utils import run_bass_kernel_spmd as _run

    a = {k: np.asarray(v) for k, v in inputs.items()}
    q_cols = np.concatenate([np.r_[c * 64:c * 64 + 64, (c + 4) * 64:(c + 4) * 64 + 64] for c in range(4)])
    db0 = 512 + 256 + 768
    in_cols = np.concatenate([q_cols, np.arange(512, db0), np.arange(db0 + 8, 2312)])
    out_rows = np.concatenate([q_cols, np.arange(512, 1024)])

    tiles = []
    for layer in range(DEPTH):
        tiles.append(_tiles(a["w_in"][layer][:, in_cols]))
        tiles.append(_tiles(a["w_out"][layer][out_rows]))
        if layer == 0:
            g, u = _tiles(a["ffn_w_gate"][0]), _tiles(a["ffn_w_up"][0])
            tiles.append(np.stack([g, u], 1).reshape(-1, P, D))
    for e in range(NE):
        g, u = _tiles(a["moe_w_gate"][0, e]), _tiles(a["moe_w_up"][0, e])
        tiles.append(np.stack([g, u], 1).reshape(-1, P, D))
        tiles.append(_tiles(a["moe_w_down"][0, e]))
    tiles.append(np.zeros((2, P, D), np.float32))
    w8 = np.concatenate(tiles)
    wd = _tiles(a["ffn_w_down"][0]).reshape(DC, P, 2, KD * P)
    w11 = wd.transpose(0, 2, 1, 3).reshape(2 * DC, P, KD * P)

    ada = a["ada_w"].reshape(4, DC, P, 12, 256).transpose(0, 3, 2, 1, 4).reshape(48, P, DC * 256)

    params = np.zeros((P, N_PAR), np.float32)

    def put(name, v):
        lo, hi = P_COLS[name]
        params[:v.shape[0], lo:hi] = v.reshape(v.shape[0], hi - lo)

    put("adab", _chunks(a["ada_b"].reshape(-1)))
    put("ng", _chunks(np.stack([a["norm_mix_g"], a["norm_ffn_g"]], 1).reshape(-1)))
    put("fg", _chunks(a["final_norm_g"]))
    put("c", _chunks(a["c"][0]))
    put("wba", a["w_in"][:, :, db0:db0 + 8].reshape(DEPTH, DC, P, 8).transpose(2, 0, 1, 3))
    for name, key in (("dtb", "dn_dt_bias"), ("alog", "dn_a_log")):
        lo, hi = P_COLS[name]
        params[4:8, lo:hi] = a[key].T
    put("sink", np.broadcast_to(a["attn_sinks"].reshape(1, -1), (P, DEPTH * 8)))
    put("dconv", a["dn_conv_w"].reshape(DEPTH, DN_CONV, 6, P).transpose(3, 0, 2, 1))
    put("dng", np.tile(a["dn_norm_g"].T, (2, 1)))
    put("cconv", a["cv_dw_w"].reshape(DEPTH, CV_K, 2, P).transpose(3, 0, 2, 1))
    for name, key in (("cb", "cv_dw_b"), ("lng", "cv_ln_g"), ("lnb", "cv_ln_b")):
        put(name, a[key].reshape(DEPTH, 2, P).transpose(2, 0, 1))
    put("rw", a["router_w"][0].reshape(DC, P, NE).transpose(1, 0, 2))
    put("rb", np.broadcast_to(a["router_b"], (P, NE)))

    arrays = {
        "xT": a["x"][0].T, "consts": constants(), "params": params, "pos": a["positions"],
        "ada": ada, "w8": w8, "w11": w11,
    }
    nc = _bacc.Bacc("TRN2", target_bir_lowering=False, num_devices=1)
    arrays = {k: np.ascontiguousarray(v) for k, v in arrays.items()}
    args = [nc.dram_tensor(f"in_{k}", v.shape, mybir.dt.from_np(v.dtype), kind="ExternalInput").ap()
            for k, v in arrays.items()]
    out = nc.dram_tensor("out_T", (D, S), F32, kind="ExternalOutput").ap()
    trunk(nc, *args, out)
    r = _run(nc, [{f"in_{k}": v for k, v in arrays.items()}], core_ids=[0])
    return np.ascontiguousarray(r.results[0]["out_T"].T)[None]
```

```python
import numpy as np

import concourse.bass as bass
from concourse import mybir
from contextlib import ExitStack

F32 = mybir.dt.float32
F32R = mybir.dt.float32r
I32 = mybir.dt.int32
ALU = mybir.AluOpType
ACT = mybir.ActivationFunctionType
AX = mybir.AxisListType

P = 128
D = 1024
S = 512
DC = D // P
DEPTH = 2
HD = 64
HQ, HKV = 8, 2
ROT = HD // 4
DN_CONV, DN_CHUNK = 4, 64
NCH = S // DN_CHUNK
NU = 2 * NCH
CV_K = 31
D_FF = 2816
FC = D_FF // P
NE = 8
FE = 1024 // P
N_IN_TILES = 18
EPS = 1e-6
NEG = -1.0e30

Q0, K0, V0, DQ, DK, DV, DZ, CA, CB = 0, 4, 5, 6, 8, 10, 12, 14, 16

C_COLS = {}
_at = 0
for _n, _w in (("ident", 128), ("ones", 128), ("bones", 128), ("rot", 128), ("istk", 64), ("amask", 256),
               ("mincT", 64), ("bd", 128), ("lev", 6 * 128), ("lev1c", 64), ("reset", 512),
               ("selb", 256), ("selg", 256), ("invf", 1), ("rotm", 1), ("nrotm", 1),
               ("eps", 1), ("eps64", 1), ("rank", 8), ("before", 128), ("iota", 128), ("part", 1), ("blocks", 16 * 8)):
    C_COLS[_n] = (_at, _at + _w)
    _at += _w
N_CONST = _at

P_COLS = {}
_at = 0
for _n, _w in (("adab", 96), ("ng", 4 * DC), ("fg", DC), ("c", DC), ("wba", DEPTH * DC * 8), ("dtb", DEPTH),
               ("alog", DEPTH), ("sink", DEPTH * 8), ("dconv", DEPTH * 6 * 4), ("dng", DEPTH),
               ("cconv", DEPTH * 2 * CV_K), ("cb", DEPTH * 2), ("lng", DEPTH * 2), ("lnb", DEPTH * 2),
               ("rw", DC * NE), ("rb", NE)):
    P_COLS[_n] = (_at, _at + _w)
    _at += _w
N_PAR = _at

T_IN = [0, 70 + 16]
T_OUT = [18, 70 + 16 + 18]
T_GU0 = 26
T_DN0 = 70
T_MOE = 70 + 16 + 26
NB = 2 * S // P + NE - 1
NT = 24
NUN = NT // 2
UNITS = [("g", 0, 0), ("g", 0, 4), ("u", 0, 0), ("u", 0, 4), ("g", 1, 0), ("g", 1, 4), ("u", 1, 0), ("u", 1, 4),
         ("d", 0, 0), ("d", 1, 0), ("d", 0, 4), ("d", 1, 4)]
KD = FC // 2
U_IN = [1, 1 + 9 + 4 + 22 + 4]
U_OUT = [1 + 9, U_IN[1] + 9]
U_GU0 = U_OUT[0] + 4
U_DN0 = U_GU0 + 22
U_MOE = U_OUT[1] + 4
X_USES = [1, U_GU0, U_IN[1], U_MOE]


def constants():
    c = np.zeros((P, N_CONST), np.float32)

    def put(name, a):
        lo, hi = C_COLS[name]
        c[:a.shape[0], lo:hi] = a.reshape(a.shape[0], hi - lo)

    p = np.arange(P)
    j64 = np.arange(64)
    put("ident", np.eye(P))
    put("ones", np.ones((P, P)))
    same = (p[:, None] // 64 == p[None, :] // 64)
    put("bones", same * 1.0)
    rot = np.zeros((P, P))
    for b in (0, 64):
        for d in range(ROT // 2):
            rot[b + d + ROT // 2, b + d] = -1.0
            rot[b + d, b + d + ROT // 2] = 1.0
    put("rot", rot)
    put("istk", (p[:, None] % 64 == j64[None, :]) * 1.0)
    diff = p[:, None] + P - np.arange(2 * P)[None, :]
    put("amask", np.where((diff >= 0) & (diff < P), 0.0, NEG))
    put("mincT", np.where(j64[None, :] >= p[:, None] % 64, 0.0, NEG))
    put("bd", same * 1.0)
    lev = np.zeros((P, 6, P))
    for n in range(6):
        s = 1 << n
        row, col = p[None, :] % 64, p[:, None] % 64
        lev[:, n] = same & (row // (2 * s) == col // (2 * s)) & (row // s % 2 == 1) & (col // s % 2 == 0)
    put("lev", lev)
    put("lev1c", ((j64[None, :] // 2 == p[:, None] % 64 // 2) & (j64[None, :] % 2 == 1) & (p[:, None] % 2 == 0)) * 1.0)
    put("reset", np.tile((np.arange(S) % 64 != 0) * 1.0, (P, 1)))
    selb, selg = np.zeros((8, 2, P)), np.zeros((8, 2, P))
    for hp in range(2):
        for par in range(2):
            selb[hp * 2 + par, hp, par * 64:par * 64 + 64] = 1.0
            selg[4 + hp * 2 + par, hp, par * 64:par * 64 + 64] = 1.0
    put("selb", selb)
    put("selg", selg)
    inv = np.float32(500000.0) ** (-np.arange(0, ROT, 2, dtype=np.float32) / np.float32(ROT))
    d = p % 64
    put("invf", np.where(d < ROT, inv[d % (ROT // 2)], 0.0)[:, None])
    put("rotm", (d < ROT)[:, None] * 1.0)
    put("nrotm", (d >= ROT)[:, None] * 1.0)
    put("eps", np.full((P, 1), EPS))
    put("eps64", np.full((P, 1), 64 * EPS))
    put("rank", np.tile(8.0 - np.arange(8), (P, 1)))
    put("before", (p[:, None] < p[None, :]) * 1.0)
    put("iota", np.tile(p * 1.0, (P, 1)))
    put("part", p[:, None] * 1.0)
    put("blocks", np.tile(np.repeat(np.arange(16.0), 8), (P, 1)))
    return c



def trunk(nc, xT, consts, params, pos, ada, w8, w11, wm, outT):
    ctx = ExitStack()
    with ctx:
        def sb(name, shape, dt=F32, stack=ctx):
            return stack.enter_context(nc.sbuf_tensor(name, [P] + shape, dt))

        sems = {}

        def sem(name):
            if name not in sems:
                sems[name] = ctx.enter_context(nc.semaphore(name))
            return sems[name]

        cst = sb("cst", [N_CONST])
        par = sb("par", [N_PAR])
        x = sb("x", [DC, S])
        hhi = sb("hhi", [DC, S], F32R)
        hlo = sb("hlo", [DC, S], F32R)
        raw = sb("raw", [2, KD * P])
        whi = sb("whi", [2, KD * P], F32R)
        wlo = sb("wlo", [2, KD * P], F32R)
        mod = sb("mod", [96])
        sclg = sb("sclg", [4, DC])
        small = sb("small", [256])
        cosb = sb("cosb", [S])
        sinb = sb("sinb", [S])
        rstd = sb("rstd", [S])
        with ExitStack() as room:
            scr = sb("scr", [17 * 1024], stack=room)
            proj = sb("proj", [N_IN_TILES, S], stack=room)
        with ExitStack() as room:
            adar = sb("adar", [4, DC * 256], stack=room)
            posi = sb("posi", [S], I32, stack=room)
            ang = sb("ang", [4, S], stack=room)
            cact = sb("cact", [DC], stack=room)
            adac = sb("adac", [4, 256], stack=room)
        with ExitStack() as room:
            ghi = sb("ghi", [FC, S], F32R, stack=room)
            glo = sb("glo", [FC, S], F32R, stack=room)
            sg = sb("sg", [S], stack=room)
            gt = sb("gt", [S], stack=room)
        with ExitStack() as room:
            rawm = sb("rawm", [3, 4 * S], stack=room)
            whm = sb("whm", [4, 2 * S], F32R, stack=room)
            wlm = sb("wlm", [4, 2 * S], F32R, stack=room)
            xgh = sb("xgh", [DC, P], F32R, stack=room)
            xgl = sb("xgl", [DC, P], F32R, stack=room)
            hih = sb("hih", [FE, P], F32R, stack=room)
            hil = sb("hil", [FE, P], F32R, stack=room)
            yh = sb("yh", [D], F32R, stack=room)
            yl = sb("yl", [D], F32R, stack=room)
            sgm = sb("sgm", [2, S], stack=room)
            tm = sb("tm", [2, S], stack=room)
            bc = sb("bc", [4, S], stack=room)
            G = sb("G", [4, P], F32R, stack=room)
            SC = sb("SC", [S], F32R, stack=room)
            junk = sb("junk", [S], stack=room)
            logit = sb("logit", [8 * 32], stack=room)
            rt = sb("rt", [96], stack=room)
            ebi = sb("ebi", [16], I32, stack=room)
        def rawm_tile(t):
            return rawm[:, t // 2 % 3, (t % 2) * 1024:(t % 2) * 1024 + 1024]

        def lo_counts(t):
            return (t + 1) - (t + 1) // 3, (t + 1) // 3

        h = scr[:, 0:DC * S].rearrange("p (c s) -> p c s", c=DC)
        ps = ctx.enter_context(nc.psum_tensor("ps", [P, 8, 512], F32))

        def C(name, rows=P):
            lo, hi = C_COLS[name]
            return cst[0:rows, lo:hi]

        def PR(name, n=0, w=1, rows=P):
            lo, _ = P_COLS[name]
            return par[0:rows, lo + n:lo + n + w]

        def unit(n, w=1):
            return scr[:, n * 1024:(n + w) * 1024]

        def cmp(ap):
            return ap.rearrange("p (u j) -> p u j", u=NU)

        def bdv(ap):
            return ap.rearrange("p (u a j) -> p u a j", u=NU, a=2)

        def lhs(ap, u):
            return ap[:, u * P:(u + 1) * P]

        def two(b):
            return ps[:, b:b + 2, :].rearrange("p b (u j) -> p (b u) j", j=64)

        def over2(ap):
            return ap.unsqueeze(2).broadcast_to([P, NU, 2, 64])

        def mask4(m):
            return m.rearrange("p (a j) -> p a j", a=2).unsqueeze(1).broadcast_to([P, NU, 2, 64])

        def col(ap16):
            return ap16.unsqueeze(2).broadcast_to([P, NU, 64])

        QA, KA, VA, GCJ, BJ, ET, LT, AT, VB = (unit(n) for n in (0, 1, 2, 3, 4, 5, 6, 7, 8))
        KBD, VBD, KBG, KG = unit(9, 2), unit(11, 2), unit(13, 2), unit(15, 2)
        TT, TC = unit(3), unit(4)
        MT, TTBD, XBD = unit(9, 2), unit(11, 2), unit(1, 2)
        UC, WBD = unit(5), unit(13, 2)
        ST, STBD = unit(3)[:, 0:128], unit(3)[:, 256:512]
        VN, VNBD = unit(4)[:, 0:128], unit(4)[:, 256:512]
        gcI, bI, egl, t16, sI, kgI = (small[:, n * 16:n * 16 + 16] for n in range(6))
        mx, negm, esk, den, rden, rsum = ([small[:, 96 + 48 * a + 8 * n:104 + 48 * a + 8 * n] for a in range(2)]
                                          for n in range(6))
        SM = [unit(3 + 2 * a, 2).rearrange("p (h k) -> p h k", h=8) for a in range(2)]
        EX = [unit(7 + 2 * a, 2).rearrange("p (h k) -> p h k", h=8) for a in range(2)]
        PT = unit(11).rearrange("p (c k q) -> p c k q", c=4, k=2)
        VTOK = unit(12)[:, 0:512].rearrange("p (n d) -> p n d", n=4)
        CTMP = unit(12)[:, 512:1024]
        ROTT = unit(13, 3)[:, 0:5 * S].rearrange("p (c s) -> p c s", c=5)
        BA = unit(16)[0:8, 0:512]
        BROW = unit(14)[0:8, 512:1024]
        GROW = unit(15)[0:8, 0:512]
        GTMP = unit(15)[0:8, 512:1024]

        DCONV_STEPS = 6 * (2 * DN_CONV - 1)

        block = ctx.enter_context(nc.Block())

        @block.sync
        def _(sp):
            sp.dma_start(cst[:], consts).then_inc(sem("inputs_in"), 16)
            sp.dma_start(par[:], params).then_inc(sem("inputs_in"), 16)
            sp.dma_start(x[:], xT.rearrange("(c p) s -> p c s", p=P)).then_inc(sem("inputs_in"), 16)
            sp.dma_start(posi[:], pos.partition_broadcast(P)).then_inc(sem("inputs_in"), 16)

            def load_ada(i, j, first=False):
                if not first:
                    sp.wait_ge(sem("ada_acc"), 4 * i + j - 3)
                sp.dma_start(adar[:, j, :], ada[bass.ds(4 * i + j, 1), :, :].rearrange("a p n -> p (a n)"))\
                    .then_inc(sem(f"ada_in{j}"), 16)

            for j in range(4):
                load_ada(0, j, True)
            for j in range(2):
                sp.dma_start(raw[:, j, 0:DC * P], w8[j, :, :]).then_inc(sem(f"tile_in{j}"), 16)
            with sp.Fori(1, 12) as i:
                for j in range(4):
                    load_ada(i, j)

            def load_tile(src, n, slot, g, width):
                sp.wait_ge(sem("lo_ready"), g - 1)
                sp.dma_start(raw[:, slot, 0:width], src[bass.ds(n, 1), :, :].rearrange("a p n -> p (a n)"))\
                    .then_inc(sem(f"tile_in{slot}"), 16)

            with sp.Fori(1, T_DN0 // 2) as i:
                for j in range(2):
                    load_tile(w8, 2 * i + j, j, 2 * i + j, DC * P)
            with sp.Fori(0, 8) as i:
                for j in range(2):
                    load_tile(w11, 2 * i + j, j, 2 * i + j + T_DN0, KD * P)
            with sp.Fori(0, (T_MOE + 2 - T_DN0 - 16) // 2) as i:
                for j in range(2):
                    load_tile(w8, 2 * i + j + T_DN0, j, 2 * i + j + T_DN0 + 16, DC * P)
            sp.wait_ge(sem("htok_lo"), 4)

            def load_unit(b, expert, u, first=False):
                at = expert * NUN + u
                if not isinstance(at, int):
                    at = sp.snap(at, min_val=0, max_val=NE * NUN - 1)
                if not first:
                    back, t = (0, 2 * (u - 3) + 1) if u >= 3 else (1, 2 * (u + NUN - 3) + 1)
                    nd, npool = lo_counts(t)
                    split = 16 * (b - back) + nd
                    sp.wait_ge(sem("lom_dve"), split)
                    sp.wait_ge(sem("lom_pool"), split)
                sp.dma_start(rawm[:, u % 3, :], wm[bass.ds(at, 1), :, :].rearrange("a p n -> p (a n)"))\
                    .then_inc(sem(f"unit_in{u % 3}"), 16)

            sp.wait_ge(sem("eb_ready"), 1)
            first = sp.value_load(ebi[0:1, 0:1], min_val=0, max_val=NE - 1)
            for u in range(NUN):
                load_unit(0, first, u, u < 3)
            with sp.Fori(1, NB) as b:
                expert = sp.value_load(ebi[0:1, bass.ds(b, 1)], min_val=0, max_val=NE - 1)
                for u in range(NUN):
                    load_unit(b, expert, u)
            for u in range(2):
                load_unit(NB, 0, u)
            sp.wait_ge(sem("out_ready"), DC)
            sp.dma_start(outT.rearrange("(c p) s -> p c s", p=P), h).then_inc(sem("stored"), 16)
            sp.wait_ge(sem("stored"), 16)

        @block.gpsimd
        def _(pool):
            for name in ("bank_free0", "bank_free1", "glo_ready"):
                pool.sem_inc(sem(name), 1)
            pool.sem_inc(sem("tilem_done"), 4)
            pool.sem_inc(sem("xm_done"), DC)
            steps = 0
            for layer in range(DEPTH):
                for j in range(2):
                    pool.wait_ge(sem(f"bank_free{j}"), U_IN[layer] + 9)
                pool.wait_ge(sem("ba_copied"), layer + 1)
                pool.wait_ge(sem("h_ready"), 16 * layer + 8)
                for n in range(6):
                    o = unit(0, 3)[:, n * S:(n + 1) * S]
                    src = proj[:, DQ + n, :]
                    for d in range(DN_CONV):
                        w = PR("dconv", (layer * 6 + n) * 4 + DN_CONV - 1 - d)
                        if d == 0:
                            pool.tensor_scalar(o, src, w, None, ALU.mult).then_inc(sem("dconv_step"), 1)
                        else:
                            pool.tensor_scalar(CTMP[:, d:], src[:, :S - d], w, None, ALU.mult).then_inc(sem("dconv_step"), 1)
                            pool.wait_ge(sem("dconv_step"), steps + 1)
                            pool.tensor_tensor(o[:, d:], o[:, d:], CTMP[:, d:], ALU.add).then_inc(sem("dconv_step"), 1)
                            steps += 1
                        steps += 1
                        pool.wait_ge(sem("dconv_step"), steps)
            def low(b, t):
                pool.wait_ge(sem("him_ready"), NT * b + t + 1)
                pool.tensor_tensor(wlm[:, t % 4, :], rawm_tile(t), whm[:, t % 4, :].bitcast(F32), ALU.subtract)\
                    .then_inc(sem("lom_pool"), 2)

            with pool.Fori(0, NB) as b:
                for t in range(2, NT, 3):
                    low(b, t)
            low(NB, 2)

        @block.tensor
        def _(pe):
            pe.wait_ge(sem("inputs_in"), 64)
            with pe.Fori(0, 12) as i:
                for j in range(4):
                    pe.wait_ge(sem("ada_acc"), 4 * i + j + 1)
                    for m in range(2):
                        ins = pe.matmul(ps[:, 7, bass.ds(8 * i + 2 * j + m, 1)], adac[:, j, m * P:m * P + P],
                                        C("ones")[:, 0:1], start=True, stop=True)
                    ins.then_inc(sem("ada_used"), 1)

            def squares(s):
                pe.wait_ge(sem("sq_ready"), s + 1)
                for k in range(DC):
                    ins = pe.matmul(ps[:, 2, :], C("ones"), h[:, k, :], start=(k == 0), stop=(k == DC - 1))
                ins.then_inc(sem("ssum_ready"), 1)

            def tile(g, slot, b, rhs_hi, rhs_lo, k0, kn, start, stop):
                pe.wait_ge(sem("lo_ready"), g + 1)
                n = 0
                for k in range(kn):
                    w_hi = whi[:, slot, k * P:(k + 1) * P]
                    w_lo = wlo[:, slot, k * P:(k + 1) * P]
                    for a, r in ((w_hi, rhs_hi), (w_hi, rhs_lo), (w_lo, rhs_hi)):
                        ins = pe.matmul(ps[:, b, :], a, r[:, k0 + k, :], start=(start and n == 0),
                                        stop=(stop and n == 3 * kn - 1))
                        n += 1
                ins.then_inc(sem("tile_done"), 1)

            def pairs(iters, g0, u0, rhs_hi, rhs_lo, base=0, ubase=0, hidden=None):
                with pe.Fori(0, iters) as i:
                    for j in range(2):
                        if hidden is not None and j == 0:
                            pe.wait_ge(sem("glo_ready"), hidden)
                        pe.wait_ge(sem(f"bank_free{j}"), u0 + ubase + i)
                        tile(g0 + base + 2 * i + j, j, j, rhs_hi, rhs_lo, 0, DC, True, True)

            def h_ready(s):
                pe.wait_ge(sem("h_ready"), 8 * s + 8)

            for layer in range(DEPTH):
                v = layer + 1
                squares(2 * layer)
                h_ready(2 * layer)
                for k in range(DC):
                    ins = pe.matmul(ps[0:8, 3, :], PR("wba", (layer * DC + k) * 8, 8), h[:, k, :],
                                    start=(k == 0), stop=(k == DC - 1))
                ins.then_inc(sem("ba_done"), 1)
                pairs(9, T_IN[layer], U_IN[layer], hhi, hlo)
                for j in range(2):
                    pe.wait_ge(sem(f"bank_free{j}"), U_IN[layer] + 9)
                pe.wait_ge(sem("ba_copied"), v)
                for n in range(5):
                    ins = pe.matmul(ps[:, 2 + n, :], C("rot"), proj[:, n, :], start=True, stop=True)
                ins.then_inc(sem("rot_done"), 1)
                for n in range(4):
                    ins = pe.transpose(ps[:, 7, n * P:(n + 1) * P], proj[:, V0, n * P:(n + 1) * P], C("ident"))
                ins.then_inc(sem("vt_done"), 1)
                pe.wait_ge(sem("rope_done"), v)
                pe.wait_ge(sem("vtok_ready"), v)
                def scores(n):
                    q = slice(n * P, (n + 1) * P)
                    lo = P if n == 0 else 0
                    if n:
                        pe.wait_ge(sem("sm_ready"), 4 * layer + n)
                    for a in range(2):
                        r = slice(64 * a, 64 * a + 64)
                        for c in range(4):
                            ins = pe.matmul(ps[:, 2 * a + c // 2, (c % 2) * 256 + lo:(c % 2) * 256 + 256],
                                            proj[r, Q0 + c, q], proj[r, K0, (n - 1) * P + lo:(n + 1) * P],
                                            start=True, stop=True)
                    ins.then_inc(sem("scores_done"), 1)

                scores(0)
                for n in range(4):
                    lo = P if n == 0 else 0
                    if n < 3:
                        scores(n + 1)
                    pe.wait_ge(sem("probs_ready"), 4 * layer + n + 1)
                    for a in range(2):
                        m = 2 * (4 * layer + n) + a
                        if m:
                            pe.wait_ge(sem("pt_ready"), m)
                        for c in range(4):
                            for kb in range(lo // P, 2):
                                ins = pe.transpose(ps[:, 4 + c // 2, (c % 2) * 256 + kb * P:(c % 2) * 256 + kb * P + P],
                                                   EX[n % 2][:, 4 * a + c, kb * P:(kb + 1) * P], C("ident"))
                        ins.then_inc(sem("pt_done"), 1)
                        pe.wait_ge(sem("pt_ready"), m + 1)
                        if a == 0 and 4 * layer + n:
                            pe.wait_ge(sem("ya_ready"), 4 * layer + n)
                        for c in range(4):
                            for kb in range(lo // P, 2):
                                ins = pe.matmul(ps[64 * a:64 * a + 64, 6, c * P:(c + 1) * P],
                                                VTOK[:, n - 1 + kb, 64 * a:64 * a + 64], PT[:, c, kb, :],
                                                start=(kb == lo // P), stop=(kb == 1))
                        ins.then_inc(sem("pv_done"), 1)
                pe.wait_ge(sem("dn_sq_ready"), v)
                pe.wait_ge(sem("ya_ready"), 4 * v)
                for n in range(4):
                    ins = pe.matmul(ps[:, 2 + n, :], C("bones"), unit(9, 2)[:, n * S:(n + 1) * S], start=True, stop=True)
                ins.then_inc(sem("dn_ss_done"), 1)
                pe.wait_ge(sem("beta_rows"), v)
                pe.wait_ge(sem("gate_rows"), v)
                for hp in range(2):
                    pe.matmul(ps[:, 6 + hp, :], C("selb", 8)[:, hp * P:(hp + 1) * P], BROW, start=True, stop=True)
                for hp in range(2):
                    ins = pe.matmul(ps[:, hp, :], C("selg", 8)[:, hp * P:(hp + 1) * P], GROW, start=True, stop=True)
                ins.then_inc(sem("rows_spread"), 1)
                pe.wait_ge(sem("kv_bd_ready"), 2 * v)
                pe.wait_ge(sem("bj_ready"), v)
                pe.wait_ge(sem("gcj_ready"), 2 * v)
                for u in range(NU):
                    o = slice((u % 8) * 64, (u % 8) * 64 + 64)
                    c = slice(u * 64, u * 64 + 64)
                    pe.matmul(ps[:, u // 8, o], lhs(KBD, u), KA[:, c], start=True, stop=True)
                    pe.matmul(ps[:, 2 + u // 8, o], lhs(KBD, u), QA[:, c], start=True, stop=True)
                    pe.matmul(ps[:, 4 + u // 8, o], lhs(KBD, u), C("istk"), start=True, stop=True)
                    ins = pe.matmul(ps[:, 6 + u // 8, o], lhs(VBD, u), C("istk"), start=True, stop=True)
                ins.then_inc(sem("gram_done"), 1)
                for lv in range(1, 6):
                    m = 5 * layer + lv - 1
                    pe.wait_ge(sem("t_ready"), m + 1)
                    pe.wait_ge(sem("mt_ready"), m + 1)
                    for u in range(NU):
                        ins = pe.matmul(ps[:, 2 + u // 8, (u % 8) * 64:(u % 8) * 64 + 64], lhs(MT, u),
                                        TC[:, u * 64:u * 64 + 64], start=True, stop=True)
                    ins.then_inc(sem("x_done"), 1)
                    pe.wait_ge(sem("xbd_ready"), m + 1)
                    for u in range(NU):
                        ins = pe.matmul(ps[:, 4 + u // 8, (u % 8) * 64:(u % 8) * 64 + 64], lhs(XBD, u),
                                        TT[:, u * 64:u * 64 + 64], start=True, stop=True)
                    ins.then_inc(sem("yt_done"), 1)
                pe.wait_ge(sem("tt_final"), v)
                for u in range(NU):
                    o = slice((u % 8) * 64, (u % 8) * 64 + 64)
                    c = slice(u * 64, u * 64 + 64)
                    pe.matmul(ps[:, u // 8, o], lhs(TTBD, u), VB[:, c], start=True, stop=True)
                    ins = pe.matmul(ps[:, 2 + u // 8, o], lhs(KBG, u), TT[:, c], start=True, stop=True)
                ins.then_inc(sem("uw_done"), 1)
                for n in range(NCH):
                    m = NCH * layer + n
                    pe.wait_ge(sem("state_ready"), (NCH + 1) * layer + n + 1)
                    for hp in range(2):
                        ins = pe.matmul(ps[:, 4, hp * 64:hp * 64 + 64], lhs(WBD, hp * 8 + n), ST[:, hp * 64:hp * 64 + 64],
                                        start=True, stop=True)
                    ins.then_inc(sem("ws_done"), 1)
                    pe.wait_ge(sem("vnew_ready"), m + 1)
                    for hp in range(2):
                        u = hp * 8 + n
                        ins = pe.matmul(ps[:, 5, hp * 64:hp * 64 + 64], lhs(KG, u), VN[:, hp * 64:hp * 64 + 64],
                                        start=True, stop=True)
                    ins.then_inc(sem("kv_done"), 1)
                    for hp in range(2):
                        u = hp * 8 + n
                        pe.matmul(ps[:, 6 + hp, n * 64:n * 64 + 64], STBD[:, hp * P:(hp + 1) * P], QA[:, u * 64:u * 64 + 64],
                                  start=True, stop=False)
                        ins = pe.matmul(ps[:, 6 + hp, n * 64:n * 64 + 64], VNBD[:, hp * P:(hp + 1) * P],
                                        AT[:, u * 64:u * 64 + 64], start=False, stop=True)
                    ins.then_inc(sem("o_done"), 1)
                pe.wait_ge(sem("osq_ready"), v)
                for hp in range(2):
                    ins = pe.matmul(ps[:, hp, :], C("bones"), unit(9)[:, hp * S:(hp + 1) * S], start=True, stop=True)
                ins.then_inc(sem("oss_done"), 1)
                for n in range(2):
                    pe.wait_ge(sem(f"tap{n}"), CV_K * v)
                for n in range(2):
                    ins = pe.matmul(ps[:, 2, :], C("ones"), proj[:, 6 + n, :], start=(n == 0), stop=(n == 1))
                ins.then_inc(sem("cmean_done"), 1)
                pe.wait_ge(sem("csq_ready"), v)
                for n in range(2):
                    ins = pe.matmul(ps[:, 3, :], C("ones"), proj[:, CB + n, :], start=(n == 0), stop=(n == 1))
                ins.then_inc(sem("cvar_done"), 1)
                pe.wait_ge(sem("ylo_ready"), v)
                pairs(4, T_OUT[layer], U_OUT[layer], hhi, hlo)
                squares(2 * layer + 1)
                if layer == 0:
                    h_ready(1)
                    pairs(FC, T_GU0, U_GU0, hhi, hlo)
                    pe.wait_ge(sem("glo_ready"), 1 + FC)
                    with pe.Fori(0, 4) as i:
                        for j in range(2):
                            pe.wait_ge(sem(f"bank_free{j}"), U_DN0 + i)
                            for half in range(2):
                                tile(T_DN0 + 4 * i + 2 * j + half, half, j, ghi, glo, half * KD, KD,
                                     half == 0, half == 1)
                else:
                    pe.wait_ge(sem("hs_ready"), 4 * DC)
                    for t in range(4):
                        for k in range(DC):
                            ins = pe.matmul(ps[:, 3, t * NE:(t + 1) * NE], h[:, k, t * P:(t + 1) * P],
                                            PR("rw", k * NE, NE), start=(k == 0), stop=(k == DC - 1))
                    ins.then_inc(sem("logits_done"), 1)
                    for c in range(4):
                        if c >= 2:
                            pe.wait_ge(sem("htok_lo"), c - 1)
                        for k in range(DC):
                            ins = pe.transpose(ps[:, 6 * (c % 2) + k // 4, (k % 4) * P:(k % 4) * P + P],
                                               h[:, k, c * P:(c + 1) * P], C("ident"))
                        ins.then_inc(sem("htok_done"), 1)
                    pe.wait_ge(sem("sel_ready"), 1)
                    sel = logit[:, 224:256]
                    for c in range(4):
                        for c2 in range(c + 1):
                            pe.matmul(ps[:, 4, c * NE:(c + 1) * NE], C("before") if c2 == c else C("ones"),
                                      sel[:, c2 * NE:(c2 + 1) * NE], start=(c2 == 0), stop=(c2 == c))
                    for c in range(4):
                        ins = pe.matmul(ps[:, 5, 0:NE], C("ones"), sel[:, c * NE:(c + 1) * NE], start=(c == 0), stop=(c == 3))
                    ins.then_inc(sem("ranks_done"), 1)
                    for q in range(4):
                        pe.wait_ge(sem("diag_ready"), q + 1)
                        if q:
                            pe.wait_ge(sem("bc_ready"), q)
                        pe.matmul(ps[:, 2, :], C("ones"), junk[:], start=True, stop=True).then_inc(sem("bc_done"), 1)

                    def gather(b):
                        pe.wait_ge(sem("G_ready"), 1 + b)
                        for half, part in ((0, hhi), (2, hlo)):
                            tok = part[:].rearrange("p c s -> p (c s)").rearrange("p (c d) -> p c d", c=4)
                            for k in range(DC):
                                for c in range(4):
                                    ins = pe.matmul(ps[:, half + k // 4, (k % 4) * P:(k % 4) * P + P],
                                                    tok[:, c, k * P:(k + 1) * P], G[:, c, :], start=(c == 0), stop=(c == 3))
                            ins.then_inc(sem("gather_done"), 1)

                    def scatter(chunks, b):
                        for n in chunks:
                            if n >= 4:
                                pe.wait_ge(sem("xm_done"), DC * b + DC + n - 3)
                            pe.matmul(ps[:, 4 + n % 4, :], yh[:, n * P:(n + 1) * P], SC[:], start=True, stop=False)
                            pe.matmul(ps[:, 4 + n % 4, :], yl[:, n * P:(n + 1) * P], SC[:], start=False, stop=True)\
                                .then_inc(sem("scatter_done"), 1)

                    def turn(b, half):
                        pe.wait_ge(sem("tm_ready"), 2 * b + half + 1)
                        for q in range(4):
                            ins = pe.transpose(ps[:, 4 + half, q * P:(q + 1) * P], tm[:, half, q * P:(q + 1) * P], C("ident"))
                        ins.then_inc(sem("turn_done"), 1)

                    pe.wait_ge(sem("htok_lo"), 4)
                    gather(0)
                    with pe.Fori(0, NB) as b:
                        for t in range(NT):
                            what, half, k0 = UNITS[t // 2]
                            k0 += 2 * (t % 2)
                            if t == 0:
                                pe.wait_ge(sem("xgh_ready"), b + 1)
                                pe.wait_ge(sem("xgl_ready"), b + 1)
                            if t == 4:
                                pe.wait_ge(sem("y_ready"), b + 1)
                                pe.wait_ge(sem("SC_ready"), b + 1)
                                scatter(range(0, 4), b)
                            if t == 8:
                                scatter(range(4, 8), b)
                            if t == 12:
                                pe.wait_ge(sem("xm_done"), DC * b + 2 * DC)
                                turn(b, 0)
                            if t == 16:
                                pe.wait_ge(sem("hil_ready"), 2 * b + 1)
                            if t == 20:
                                turn(b, 1)
                                gather(b + 1)
                                pe.wait_ge(sem("hil_ready"), 2 * b + 2)
                            nd, npool = lo_counts(t)
                            if t % 3 == 2:
                                pe.wait_ge(sem("lom_pool"), 16 * b + 2 * npool)
                            else:
                                pe.wait_ge(sem("lom_dve"), 16 * b + nd)
                            bank = {"g": 2 * half, "u": 2 * half + 1, "d": 6 + half}[what]
                            ah, al = (hih, hil) if what == "d" else (xgh, xgl)
                            for q in range(2):
                                k = k0 + q
                                w_hi = whm[:, t % 4, q * S:(q + 1) * S]
                                w_lo = wlm[:, t % 4, q * S:(q + 1) * S]
                                pe.matmul(ps[:, bank, :], ah[:, k, :], w_hi, start=(k == 0), stop=False)
                                pe.matmul(ps[:, bank, :], ah[:, k, :], w_lo, start=False, stop=False)
                                ins = pe.matmul(ps[:, bank, :], al[:, k, :], w_hi, start=False, stop=(k == DC - 1))
                            ins.then_inc(sem("tilem_done"), 1)
                    pe.wait_ge(sem("y_ready"), NB + 1)
                    pe.wait_ge(sem("SC_ready"), NB + 1)
                    scatter(range(DC), NB)
            squares(4)

        @block.scalar
        def _(act):
            count = {}

            def mark(ins, name, n=1):
                count[name] = count.get(name, 0) + n
                ins.then_inc(sem(name), 1)
                act.wait_ge(sem(name), count[name])

            def split(slot, g, use, width=DC * P):
                act.wait_ge(sem(f"tile_in{slot}"), use)
                if not (isinstance(g, int) and g < 2):
                    act.wait_ge(sem("tile_done"), g - 1)
                act.activation(whi[:, slot, 0:width], raw[:, slot, 0:width], ACT.Copy).then_inc(sem("hi_ready"), 1)

            def use_of(g_half):
                return 16 * g_half + 16

            def norm(s):
                if s == 4:
                    act.wait_ge(sem("xm_done"), DC * (NB + 2))
                    act.wait_ge(sem("lom_pool"), 16 * NB + 2)
                    act.wait_ge(sem("lom_dve"), 16 * NB + 3)
                elif s:
                    for j in range(2):
                        act.wait_ge(sem(f"bank_free{j}"), X_USES[s])
                act.activation(h, x[:], ACT.Square).then_inc(sem("sq_ready"), 1)
                act.wait_ge(sem("ssum_ready"), s + 1)
                act.activation(rstd[:], ps[:, 2, :], ACT.Sqrt, scale=1.0 / D, bias=C("eps")).then_inc(sem("rms_ready"), 1)
                if s == 4:
                    return
                for k in range(DC):
                    act.wait_ge(sem("hn_ready"), 8 * s + k + 1)
                    mark(act.activation(h[:, k, :], h[:, k, :], ACT.Identity, scale=sclg[:, s, k:k + 1],
                                        bias=mod[:, s * 24 + k:s * 24 + k + 1]), "hs_ready")
                    if s < 3:
                        act.activation(hhi[:, k, :], h[:, k, :], ACT.Copy).then_inc(sem("hhi_ready"), 1)

            act.wait_ge(sem("inputs_in"), 64)
            act.activation(cact[:, 0:DC], PR("c", 0, DC), ACT.Silu).then_inc(sem("cact_ready"), 1)
            act.wait_ge(sem("ang_ready"), 2)
            act.activation(sinb[:], ang[:, 2, :], ACT.Sin).then_inc(sem("sincos"), 1)
            act.activation(cosb[:], ang[:, 3, :], ACT.Sin).then_inc(sem("sincos"), 1)
            for g in range(2):
                split(g, g, 16)
            act.wait_ge(sem("mod_ready"), 2)

            for layer in range(DEPTH):
                v = layer + 1
                norm(2 * layer)
                g0 = T_IN[layer]
                with act.Fori(0, 9) as i:
                    for j in range(2):
                        split(j, g0 + 2 * i + j + 2, 16 * i + 8 * g0 + 32)
                        act.wait_ge(sem("tile_done"), g0 + 2 * i + j + 1)
                        act.activation(proj[:, bass.ds(2 * i + j, 1), :], ps[:, j:j + 1, :], ACT.Copy)\
                            .then_inc(sem(f"bank_free{j}"), 1)
                for j in range(2):
                    act.wait_ge(sem(f"bank_free{j}"), U_IN[layer] + 9)
                def exps(n):
                    a, lo = n % 2, P if n == 0 else 0
                    act.wait_ge(sem("mx_ready"), 4 * layer + n + 1)
                    act.wait_ge(sem("sm_ready"), 4 * layer + n + 1)
                    if n >= 2:
                        act.wait_ge(sem("pt_done"), 2 * (4 * layer + n) - 2)
                    for hd in range(8):
                        ins = act.activation(EX[a][:, hd, lo:256], SM[a][:, hd, lo:256], ACT.Exp,
                                             bias=negm[a][:, hd:hd + 1], accum_out=rsum[a][:, hd:hd + 1])
                    ins.then_inc(sem("exp_ready"), 1)
                    act.wait_ge(sem("esk_in"), 4 * layer + n + 1)
                    act.activation(esk[a], den[a], ACT.Exp).then_inc(sem("esk_ready"), 1)

                exps(0)
                for n in range(4):
                    lo = P if n == 0 else 0
                    if n < 3:
                        exps(n + 1)
                    for a in range(2):
                        act.wait_ge(sem("pt_done"), 2 * (4 * layer + n) + a + 1)
                        if a or n or layer:
                            act.wait_ge(sem("pv_done"), 2 * (4 * layer + n) + a)
                        act.activation(PT[:, :, lo // P:2, :],
                                       ps[:, 4:6, :].rearrange("p b (c k q) -> p (b c) k q", c=2, k=2)[:, :, lo // P:2, :],
                                       ACT.Copy).then_inc(sem("pt_ready"), 1)
                act.wait_ge(sem("dconv_step"), DCONV_STEPS * v)
                mark(act.activation(unit(0, 3), unit(0, 3), ACT.Silu), "dsilu_ready")
                mark(act.activation(proj[:, DZ:DZ + 2, :], proj[:, DZ:DZ + 2, :], ACT.Silu), "zsilu_ready")
                act.activation(proj[:, CB:CB + 2, :], proj[:, CB:CB + 2, :], ACT.Sigmoid).then_inc(sem("csig_ready"), 1)
                act.activation(unit(9, 2), unit(0, 2), ACT.Square).then_inc(sem("dn_sq_ready"), 1)
                act.wait_ge(sem("rows_in"), v)
                mark(act.activation(BROW, BA, ACT.Sigmoid), "beta_rows")
                act.wait_ge(sem("dn_ss_done"), v)
                act.activation(unit(11, 2)[:, 0:1024], ps[:, 2:4, :].rearrange("p b n -> p (b n)"), ACT.Sqrt,
                               scale=64.0, bias=C("eps64"))
                act.activation(unit(11, 2)[:, 1024:2048], ps[:, 4:6, :].rearrange("p b n -> p (b n)"), ACT.Sqrt,
                               bias=C("eps")).then_inc(sem("dn_norm_ready"), 1)
                mark(act.activation(GTMP, GROW, ACT.Abs), "g_abs")
                mark(act.activation(GTMP, GTMP, ACT.Exp, scale=-1.0), "g_exp")
                act.activation(GTMP, GTMP, ACT.Ln, bias=1.0).then_inc(sem("g_ln"), 1)
                act.activation(small[0:8, 200:201], PR("alog", layer, 1, 8), ACT.Exp).then_inc(sem("g_ln"), 1)
                act.wait_ge(sem("rows_spread"), v)
                act.activation(BJ, ps[:, 6:8, :].rearrange("p b n -> p (b n)"), ACT.Copy).then_inc(sem("bj_ready"), 1)
                act.wait_ge(sem("dift_ready"), v)
                act.activation(ET, ET, ACT.Exp).then_inc(sem("et_ready"), 1)
                act.wait_ge(sem("gci_ready"), v)
                act.activation(t16, gcI, ACT.Exp).then_inc(sem("egi_ready"), 1)
                act.activation(egl, cmp(GCJ)[:, :, 63], ACT.Exp).then_inc(sem("egi_ready"), 1)
                act.activation(kgI, kgI, ACT.Exp).then_inc(sem("egi_ready"), 1)
                act.wait_ge(sem("gram_done"), v)
                act.wait_ge(sem("gram_read"), v)
                act.activation(KA, GCJ, ACT.Exp).then_inc(sem("egj_ready"), 1)
                act.wait_ge(sem("uw_done"), v)
                act.activation(UC, ps[:, 0:2, :].rearrange("p b n -> p (b n)"), ACT.Copy).then_inc(sem("uc_ready"), 1)
                act.wait_ge(sem("o_done"), NCH * v)
                act.activation(unit(9), ps[:, 6:8, :].rearrange("p b n -> p (b n)"), ACT.Square).then_inc(sem("osq_ready"), 1)
                act.wait_ge(sem("oss_done"), v)
                act.activation(unit(10), ps[:, 0:2, :].rearrange("p b n -> p (b n)"), ACT.Sqrt, scale=1.0 / 64,
                               bias=C("eps")).then_inc(sem("orms_ready"), 1)
                act.wait_ge(sem("cxc_ready"), v)
                act.activation(proj[:, CB:CB + 2, :], proj[:, 6:8, :], ACT.Square).then_inc(sem("csq_ready"), 1)
                act.wait_ge(sem("cvar_done"), v)
                act.activation(rstd[:], ps[:, 3, :], ACT.Sqrt, scale=1.0 / 256, bias=C("eps")).then_inc(sem("crms_ready"), 1)
                act.wait_ge(sem("cn_ready"), v)
                for n in range(2):
                    mark(act.activation(proj[:, 6 + n, :], proj[:, 6 + n, :], ACT.Silu,
                                        scale=PR("lng", layer * 2 + n), bias=PR("lnb", layer * 2 + n)), "cy_ready")
                act.wait_ge(sem("yd_ready"), v)
                act.activation(hhi[:], proj[:, 0:8, :], ACT.Copy).then_inc(sem("yhi_ready"), 1)
                g0 = T_OUT[layer]
                with act.Fori(0, 4) as i:
                    for j in range(2):
                        split(j, g0 + 2 * i + j + 2, 16 * i + 8 * g0 + 32)
                norm(2 * layer + 1)

                def gate_up(g0, k0, u0, off=0, uoff=0):
                    def step(i, j, width):
                        split(j, g0 + off + 2 * i + j + 2, 16 * i + 8 * (g0 + off) + 32, width)

                    def one(i, width):
                        step(i, 0, width)
                        act.wait_ge(sem("tile_done"), g0 + off + 2 * i + 1)
                        act.wait_ge(sem("bank_free1"), u0 + uoff + i)
                        act.activation(sg[:], ps[:, 0, :], ACT.Silu).then_inc(sem("bank_free0"), 1)
                        step(i, 1, width)
                        act.wait_ge(sem("bank_free1"), u0 + uoff + i + 1)
                        act.activation(ghi[:, bass.ds(i, 1), :], gt[:].unsqueeze(1), ACT.Copy).then_inc(sem("ghi_ready"), 1)
                    return one

                if layer == 0:
                    one = gate_up(T_GU0, 0, U_GU0)
                    with act.Fori(0, FC - 1) as i:
                        one(i, DC * P)
                    with act.Fori(FC - 1, FC) as i:
                        one(i, KD * P)
                    with act.Fori(0, 7) as i:
                        for j in range(2):
                            split(j, T_DN0 + 2 * i + j + 2, 16 * i + 8 * T_DN0 + 32, KD * P)
                    for j in range(2):
                        split(j, T_DN0 + 16 + j, 16 * 7 + 8 * T_DN0 + 32)
                else:
                    for c in range(4):
                        act.wait_ge(sem("htok_done"), c + 1)
                        act.activation(hhi[:, 2 * c:2 * c + 2, :], ps[:, 6 * (c % 2):6 * (c % 2) + 2, :], ACT.Copy)\
                            .then_inc(sem("htok_hi"), 1)
                    act.wait_ge(sem("route_in"), 1)
                    act.activation(small[:, 212:216], small[:, 212:216], ACT.Exp).then_inc(sem("route_exp"), 1)
                    for q in range(4):
                        act.wait_ge(sem("bc_done"), q + 1)
                        act.activation(bc[:, q, :], ps[:, 2, :], ACT.Copy).then_inc(sem("bc_ready"), 1)

                    def high(b, t):
                        if t % 2 == 0:
                            act.wait_ge(sem(f"unit_in{t // 2 % 3}"), 64 * b + 16 * (t // 6) + 16)
                        act.wait_ge(sem("tilem_done"), NT * b + t + 1)
                        act.activation(whm[:, t % 4, :], rawm_tile(t), ACT.Copy).then_inc(sem("him_ready"), 1)

                    def tokens(b):
                        act.wait_ge(sem("gather_done"), 2 * b + 1)
                        act.activation(xgh[:], ps[:, 0:2, :].rearrange("p b (k s) -> p (b k) s", s=P), ACT.Copy)\
                            .then_inc(sem("xgh_ready"), 1)

                    def hidden(b, half):
                        act.wait_ge(sem("turn_done"), 2 * b + half + 1)
                        act.activation(hih[:, 4 * half:4 * half + 4, :],
                                       ps[:, 4 + half, :].rearrange("p (k s) -> p k s", s=P), ACT.Copy)\
                            .then_inc(sem("hih_ready"), 1)

                    for t in range(4):
                        high(0, t)
                    tokens(0)
                    with act.Fori(0, NB) as b:
                        for t in range(NT):
                            if t + 4 < NT:
                                high(b, t + 4)
                            else:
                                high(b + 1, t + 4 - NT)
                            if t in (3, 11):
                                act.activation(sgm[:, t // 8, :], ps[:, 2 * (t // 8), :], ACT.Silu)\
                                    .then_inc(sem("sgm_ready"), 1)
                            if t == 11:
                                hidden(b, 0)
                            if t == 19:
                                hidden(b, 1)
                                tokens(b + 1)
                            if t == 23:
                                act.wait_ge(sem("pslot_ready"), b + 1)
                                act.activation(yh[:], ps[:, 6:8, :].rearrange("p b n -> p (b n)"), ACT.Copy,
                                               scale=rt[:, 80:81]).then_inc(sem("yh_ready"), 1)
            norm(4)

        @block.vector
        def _(dve):
            count = {}
            here = [0]

            def link(ins):
                here[0] += 1
                ins.then_inc(sem("dve_step"), 1)
                dve.wait_ge(sem("dve_step"), here[0])

            def mark(ins, name):
                count[name] = count.get(name, 0) + 1
                ins.then_inc(sem(name), 1)
                dve.wait_ge(sem(name), count[name])

            def tt(out, a, b, op=ALU.mult):
                return dve.tensor_tensor(out, a, b, op)

            def stt(out, a, s, b, op0=ALU.mult, op1=ALU.add):
                return dve.scalar_tensor_tensor(out=out, in0=a, scalar=s, in1=b, op0=op0, op1=op1)

            def split(slot, g, width=DC * P):
                dve.wait_ge(sem("hi_ready"), g + 1)
                dve.tensor_tensor(wlo[:, slot, 0:width], raw[:, slot, 0:width], whi[:, slot, 0:width].bitcast(F32),
                                  ALU.subtract).then_inc(sem("lo_ready"), 1)

            def norm(s):
                dve.wait_ge(sem("rms_ready"), s + 1)
                link(dve.reciprocal(rstd[:], rstd[:]))
                if s == 4:
                    for k in range(DC):
                        stt(h[:, k, :], x[:, k, :], PR("fg", k), rstd[:], ALU.mult, ALU.mult).then_inc(sem("out_ready"), 1)
                    return
                for k in range(DC):
                    tt(h[:, k, :], x[:, k, :], rstd[:]).then_inc(sem("hn_ready"), 1)
                if s == 3:
                    return
                for k in range(DC):
                    dve.wait_ge(sem("hhi_ready"), 8 * s + k + 1)
                    tt(hlo[:, k, :], h[:, k, :], hhi[:, k, :].bitcast(F32), ALU.subtract).then_inc(sem("h_ready"), 1)

            dve.wait_ge(sem("inputs_in"), 64)
            two_pi = 2 * np.pi
            c1 = 6.28125
            c2 = float(np.float32(np.round((two_pi - c1) * 2 ** 17) / 2 ** 17))
            c3 = float(np.float32(np.round((two_pi - c1 - c2) * 2 ** 26) / 2 ** 26))
            c4 = float(np.float32(two_pi - c1 - c2 - c3))
            magic = 12582912.0
            link(dve.tensor_copy(ang[:, 0, :], posi[:]))
            link(dve.tensor_scalar(ang[:, 0, :], ang[:, 0, :], C("invf"), None, ALU.mult))
            for n, shift in ((2, 0.0), (3, 0.25)):
                link(dve.tensor_scalar(ang[:, 1, :], ang[:, 0, :], float(1 / two_pi), shift, ALU.mult, ALU.add))
                link(dve.tensor_scalar(ang[:, 1, :], ang[:, 1, :], magic, None, ALU.add))
                link(dve.tensor_scalar(ang[:, 1, :], ang[:, 1, :], magic, None, ALU.subtract))
                prev = ang[:, 0, :]
                for cc in (c1, c2, c3, c4):
                    link(stt(ang[:, n, :], ang[:, 1, :], -cc, prev))
                    prev = ang[:, n, :]
                link(dve.tensor_scalar(ang[:, n, :], ang[:, n, :], float(two_pi * shift), float(np.float32(3.1415925)),
                                       ALU.add, ALU.min))
                dve.tensor_scalar(ang[:, n, :], ang[:, n, :], -float(np.float32(3.1415925)), None, ALU.max)\
                    .then_inc(sem("ang_ready"), 1)
            dve.wait_ge(sem("sincos"), 2)
            link(dve.tensor_scalar(cosb[:], cosb[:], C("rotm"), C("nrotm"), ALU.mult, ALU.add))
            link(dve.tensor_scalar(sinb[:], sinb[:], C("rotm"), None, ALU.mult))
            for g in range(2):
                split(g, g)
            dve.wait_ge(sem("cact_ready"), 1)

            def ada_groups(i, pair, first):
                for j in pair:
                    dve.wait_ge(sem(f"ada_in{j}"), 16 * i + 16)
                    if not first:
                        dve.wait_ge(sem("ada_used"), 4 * i + j - 3)
                for k in range(DC):
                    for j in pair:
                        w = adar[:, j, k * 256:(k + 1) * 256]
                        if k == 0:
                            ins = dve.tensor_scalar(adac[:, j, :], w, cact[:, 0:1], None, ALU.mult)
                        else:
                            dve.wait_ge(sem(f"ada_step{j}"), 7 * i + k)
                            ins = stt(adac[:, j, :], w, cact[:, k:k + 1], adac[:, j, :])
                        ins.then_inc(sem("ada_acc") if k == DC - 1 else sem(f"ada_step{j}"), 1)

            for pair in ((0, 1), (2, 3)):
                ada_groups(0, pair, True)
            with dve.Fori(1, 12) as i:
                for pair in ((0, 1), (2, 3)):
                    ada_groups(i, pair, False)
            dve.wait_ge(sem("ada_used"), 48)
            mark(tt(mod[:], ps[:, 7, 0:96], PR("adab", 0, 96), ALU.add), "mod_ready")
            mark(stt(sclg[:], mod[:].rearrange("p (s t k) -> p s t k", s=4, t=3)[:, :, 1, :], 1.0,
                     PR("ng", 0, 4 * DC).rearrange("p (s k) -> p s k", s=4), ALU.add, ALU.mult), "mod_ready")

            for layer in range(DEPTH):
                v = layer + 1
                norm(2 * layer)
                g0 = T_IN[layer]
                with dve.Fori(0, 9) as i:
                    for j in range(2):
                        split(j, g0 + 2 * i + j + 2)
                dve.wait_ge(sem("ba_done"), v)
                dve.tensor_copy(BA, ps[0:8, 3, :]).then_inc(sem("ba_copied"), 1)
                dve.wait_ge(sem("rot_done"), v)
                five = lambda ap: ap.unsqueeze(1).broadcast_to([P, 5, S])
                link(tt(ROTT, ps[:, 2:7, :], five(sinb[:])))
                link(tt(proj[:, 0:5, :], proj[:, 0:5, :], five(cosb[:])))
                tt(proj[:, 0:5, :], proj[:, 0:5, :], ROTT, ALU.add).then_inc(sem("rope_done"), 1)
                dve.wait_ge(sem("vt_done"), v)
                dve.tensor_copy(VTOK, ps[:, 7, :].rearrange("p (n d) -> p n d", n=4)).then_inc(sem("vtok_ready"), 1)
                def maxima(n):
                    a, lo = n % 2, P if n == 0 else 0
                    w = 256 - lo
                    dve.wait_ge(sem("scores_done"), 4 * layer + n + 1)
                    sv = ps[:, 0:4, :].rearrange("p b (c k) -> p (b c) k", c=2)[:, :, lo:256]
                    am = C("amask")[:, lo:256].unsqueeze(1).broadcast_to([P, 8, w])
                    sinks = PR("sink", layer * 8, 8)
                    mark(stt(SM[a][:, :, lo:256], sv, HD ** -0.5, am), "sm_ready")
                    link(dve.tensor_reduce(mx[a], SM[a][:, :, lo:256], AX.X, ALU.max))
                    link(tt(mx[a], mx[a], sinks, ALU.max))
                    dve.tensor_scalar(negm[a], mx[a], -1.0, None, ALU.mult).then_inc(sem("mx_ready"), 1)
                    tt(den[a], sinks, mx[a], ALU.subtract).then_inc(sem("esk_in"), 1)

                def attended(n):
                    dve.wait_ge(sem("pv_done"), 2 * (4 * layer + n) + 2)
                    dve.tensor_copy(proj[:, 0:4, n * P:(n + 1) * P], ps[:, 6, :].rearrange("p (c q) -> p c q", c=4))\
                        .then_inc(sem("ya_ready"), 1)

                maxima(0)
                for n in range(4):
                    a, w = n % 2, P if n == 0 else 256
                    if n < 3:
                        maxima(n + 1)
                    dve.wait_ge(sem("exp_ready"), 4 * layer + n + 1)
                    dve.wait_ge(sem("esk_ready"), 4 * layer + n + 1)
                    link(tt(den[a], rsum[a], esk[a], ALU.add))
                    link(dve.reciprocal(rden[a], den[a]))
                    tt(EX[a][:, :, 256 - w:256], EX[a][:, :, 256 - w:256], rden[a].unsqueeze(2).broadcast_to([P, 8, w]))\
                        .then_inc(sem("probs_ready"), 1)
                    if n:
                        attended(n - 1)
                attended(3)
                dve.wait_ge(sem("ba_copied"), v)
                mark(dve.tensor_scalar(GROW, BA, PR("dtb", layer, 1, 8), None, ALU.add), "rows_in")
                dve.wait_ge(sem("csig_ready"), v)
                link(tt(proj[:, CA:CA + 2, :], proj[:, CA:CA + 2, :], proj[:, CB:CB + 2, :]))
                tap_list = [(d, n) for d in range(CV_K) for n in range(2)]

                def taps(m):
                    for _ in range(min(m, len(tap_list))):
                        d, n = tap_list.pop(0)
                        o = proj[:, 6 + n, :]
                        src = proj[:, CA + n, :]
                        w = PR("cconv", (layer * 2 + n) * CV_K + CV_K - 1 - d)
                        if d == 0:
                            ins = dve.tensor_scalar(o, src, w, PR("cb", layer * 2 + n), ALU.mult, ALU.add)
                        else:
                            dve.wait_ge(sem(f"tap{n}"), CV_K * layer + d)
                            ins = stt(o[:, d:], src[:, :S - d], w, o[:, d:])
                        ins.then_inc(sem(f"tap{n}"), 1)

                dve.wait_ge(sem("g_ln"), 2 * v)
                link(dve.tensor_scalar(GROW, GROW, 0.0, None, ALU.max))
                link(tt(GROW, GROW, GTMP, ALU.add))
                mark(dve.tensor_scalar(small[0:8, 201:202], small[0:8, 200:201], -1.0, None, ALU.mult), "alog_neg")
                dve.tensor_scalar(GROW, GROW, small[0:8, 201:202], None, ALU.mult).then_inc(sem("gate_rows"), 1)
                dve.wait_ge(sem("dn_norm_ready"), v)
                link(dve.reciprocal(unit(11, 2), unit(11, 2)))
                link(tt(unit(0, 2), unit(0, 2), unit(11, 2)))
                mark(tt(bdv(KBD), over2(cmp(KA)), mask4(C("bd"))), "kv_bd_ready")
                mark(tt(bdv(VBD), over2(cmp(VA)), mask4(C("bd"))), "kv_bd_ready")
                dve.wait_ge(sem("rows_spread"), v)
                for hp in range(2):
                    mark(dve.tensor_tensor_scan(GCJ[:, hp * S:(hp + 1) * S], C("reset"), ps[:, hp, :], 0.0,
                                                ALU.mult, ALU.add), "gcj_ready")
                dve.wait_ge(sem("bj_ready"), v)
                istk = C("istk").unsqueeze(1).broadcast_to([P, NU, 64])
                link(tt(cmp(LT), cmp(GCJ), istk))
                mark(dve.tensor_reduce(gcI, cmp(LT), AX.X, ALU.add), "gci_tmp")
                link(tt(cmp(LT), cmp(BJ), istk))
                link(dve.tensor_reduce(bI, cmp(LT), AX.X, ALU.add))
                link(tt(cmp(ET), cmp(GCJ), col(gcI), ALU.subtract))
                mark(tt(cmp(ET), cmp(ET), C("mincT").unsqueeze(1).broadcast_to([P, NU, 64]), ALU.add), "dift_ready")
                mark(tt(kgI, cmp(GCJ)[:, :, 63], gcI, ALU.subtract), "gci_ready")
                dve.wait_ge(sem("egi_ready"), 3 * v)
                link(tt(sI, bI, t16))
                dve.wait_ge(sem("gram_done"), v)
                dve.wait_ge(sem("et_ready"), v)
                link(tt(cmp(LT), two(0), cmp(ET)))
                link(tt(LT, LT, BJ))
                link(tt(cmp(AT), two(2), cmp(ET)))
                link(tt(cmp(ET), two(4), col(sI)))
                link(tt(bdv(KBG), over2(cmp(ET)), mask4(C("bd"))))
                link(tt(cmp(ET), two(4), col(kgI)))
                link(tt(bdv(KG), over2(cmp(ET)), mask4(C("bd"))))
                mark(tt(cmp(VB), two(6), col(bI)), "gram_read")
                dve.wait_ge(sem("egj_ready"), v)
                link(tt(QA, QA, KA))
                lev = lambda n: C("lev")[:, n * P:(n + 1) * P]
                link(tt(cmp(TT), cmp(LT), C("lev1c").unsqueeze(1).broadcast_to([P, NU, 64])))
                link(tt(cmp(TT), istk, cmp(TT), ALU.subtract))
                mark(dve.transpose(TC, TT), "t_ready")
                mark(tt(bdv(MT), over2(cmp(LT)), mask4(lev(1))), "mt_ready")
                for lv in range(1, 6):
                    m = 5 * layer + lv
                    taps(6)
                    dve.wait_ge(sem("x_done"), m)
                    mark(tt(bdv(XBD), over2(two(2)), mask4(C("bd"))), "xbd_ready")
                    if lv < 5:
                        mark(tt(bdv(MT), over2(cmp(LT)), mask4(lev(lv + 1))), "mt_ready")
                    taps(6)
                    dve.wait_ge(sem("yt_done"), m)
                    link(tt(cmp(TT), cmp(TT), two(4), ALU.subtract))
                    if lv < 5:
                        mark(dve.transpose(TC, TT), "t_ready")
                mark(tt(bdv(TTBD), over2(cmp(TT)), mask4(C("bd"))), "tt_final")
                taps(2 * CV_K)
                dve.wait_ge(sem("uw_done"), v)
                link(tt(bdv(WBD), over2(two(2)), mask4(C("bd"))))
                dve.wait_ge(sem("uc_ready"), v)
                link(dve.memset(ST, 0.0))
                mark(dve.memset(STBD, 0.0), "state_ready")
                pr2 = lambda ap: ap.rearrange("p (a j) -> p a j", a=2)
                pr4 = lambda ap: ap.rearrange("p (u a j) -> p u a j", u=2, a=2)
                bd2 = C("bd").rearrange("p (a j) -> p a j", a=2).unsqueeze(1).broadcast_to([P, 2, 2, 64])
                uc3 = UC.rearrange("p (u n j) -> p u n j", u=2, n=NCH)
                for n in range(NCH):
                    m = NCH * layer + n
                    dve.wait_ge(sem("ws_done"), m + 1)
                    if m:
                        dve.wait_ge(sem("o_done"), m)
                    link(tt(pr2(VN), uc3[:, :, n, :], ps[:, 4, 0:128].rearrange("p (a j) -> p a j", a=2), ALU.subtract))
                    mark(tt(pr4(VNBD), pr2(VN).unsqueeze(2).broadcast_to([P, 2, 2, 64]), bd2), "vnew_ready")
                    dve.wait_ge(sem("kv_done"), m + 1)
                    dve.wait_ge(sem("o_done"), m + 1)
                    for hp in range(2):
                        o = ST[:, hp * 64:hp * 64 + 64]
                        link(stt(o, o, egl[:, hp * 8 + n:hp * 8 + n + 1], ps[:, 5, hp * 64:hp * 64 + 64]))
                    mark(tt(pr4(STBD), pr2(ST).unsqueeze(2).broadcast_to([P, 2, 2, 64]), bd2), "state_ready")
                dve.wait_ge(sem("orms_ready"), v)
                link(dve.reciprocal(unit(10), unit(10)))
                dve.wait_ge(sem("osq_ready"), v)
                yd = proj[:, 4:6, :]
                link(tt(yd, ps[:, 6:8, :], unit(10).rearrange("p (a s) -> p a s", a=2)))
                dve.wait_ge(sem("zsilu_ready"), v)
                mark(stt(yd, yd, PR("dng", layer), proj[:, DZ:DZ + 2, :], ALU.mult, ALU.mult), "yd_ready")
                dve.wait_ge(sem("cmean_done"), v)
                cy = proj[:, 6:8, :]
                for n in range(2):
                    dve.wait_ge(sem(f"tap{n}"), CV_K * v)
                mark(stt(cy, ps[:, 2:3, :].broadcast_to([P, 2, S]), -1.0 / 256, cy), "cxc_ready")
                dve.wait_ge(sem("crms_ready"), v)
                link(dve.reciprocal(rstd[:], rstd[:]))
                mark(tt(cy, cy, rstd[:].unsqueeze(1).broadcast_to([P, 2, S])), "cn_ready")
                dve.wait_ge(sem("yhi_ready"), v)
                mark(tt(hlo[:], proj[:, 0:8, :], hhi[:].bitcast(F32), ALU.subtract), "ylo_ready")

                def residual(n, j, done, gate, uses):
                    dve.wait_ge(sem("tile_done"), done)
                    dve.wait_ge(sem(f"bank_free{j}"), uses)
                    stt(x[:, bass.ds(n, 1), :], ps[:, j:j + 1, :], mod[:, bass.ds(n + gate, 1)], x[:, bass.ds(n, 1), :])\
                        .then_inc(sem(f"bank_free{j}"), 1)

                g0 = T_OUT[layer]
                with dve.Fori(0, 4) as i:
                    for j in range(2):
                        split(j, g0 + 2 * i + j + 2)
                        residual(2 * i + j, j, g0 + 2 * i + j + 1, layer * 48 + 16, U_OUT[layer] + i)
                for j in range(2):
                    dve.wait_ge(sem(f"bank_free{j}"), X_USES[2 * layer + 1])
                norm(2 * layer + 1)

                def gate_up(i, g0, k0, u0, width):
                    for j in range(2):
                        split(j, g0 + 2 * i + j + 2, width)
                    dve.wait_ge(sem("tile_done"), g0 + 2 * i + 2)
                    dve.wait_ge(sem("bank_free0"), u0 + i + 1)
                    dve.wait_ge(sem("glo_ready"), k0 + i + 1)
                    tt(gt[:].unsqueeze(1), ps[:, 1:2, :], sg[:].unsqueeze(1)).then_inc(sem("bank_free1"), 1)
                    dve.wait_ge(sem("ghi_ready"), k0 + i + 1)
                    tt(glo[:, bass.ds(i, 1), :], gt[:].unsqueeze(1), ghi[:, bass.ds(i, 1), :].bitcast(F32), ALU.subtract)\
                        .then_inc(sem("glo_ready"), 1)

                if layer == 0:
                    with dve.Fori(0, FC - 1) as i:
                        gate_up(i, T_GU0, 0, U_GU0, DC * P)
                    with dve.Fori(FC - 1, FC) as i:
                        gate_up(i, T_GU0, 0, U_GU0, KD * P)

                    def down(i, widths):
                        for j in range(2):
                            for half in range(2):
                                split(half, T_DN0 + 4 * i + 2 * j + half + 2, widths[j])
                            residual(2 * i + j, j, T_DN0 + 4 * i + 2 * j + 2, 24 + 16, U_DN0 + i)

                    with dve.Fori(0, 3) as i:
                        down(i, (KD * P, KD * P))
                    with dve.Fori(3, 4) as i:
                        down(i, (KD * P, DC * P))
                    for j in range(2):
                        dve.wait_ge(sem(f"bank_free{j}"), X_USES[2])
                else:
                    def slot(n):
                        return logit[:, n * 32:(n + 1) * 32].rearrange("p (t e) -> p t e", t=4)

                    def four(n):
                        return small[:, 204 + 4 * n:208 + 4 * n]

                    def wide(ap):
                        return ap.unsqueeze(2).broadcast_to([P, 4, NE])

                    dve.wait_ge(sem("logits_done"), 1)
                    link(tt(slot(0), ps[:, 3, 0:32].rearrange("p (t e) -> p t e", t=4),
                            PR("rb", 0, NE).unsqueeze(1).broadcast_to([P, 4, NE]), ALU.add))
                    for n, (src, hot) in enumerate(((0, 3), (4, 5))):
                        link(dve.tensor_reduce(four(n), slot(src), AX.X, ALU.max))
                        link(tt(slot(1), slot(src), wide(four(n)), ALU.is_equal))
                        link(tt(slot(1), slot(1), C("rank").unsqueeze(1).broadcast_to([P, 4, NE])))
                        link(dve.tensor_reduce(four(3), slot(1), AX.X, ALU.max))
                        link(tt(slot(hot), slot(1), wide(four(3)), ALU.is_equal))
                        if n == 0:
                            link(stt(slot(4), slot(3), NEG, slot(0)))
                    mark(tt(four(2), four(1), four(0), ALU.subtract), "route_in")
                    mark(tt(slot(7), slot(3), slot(5), ALU.add), "sel_ready")
                    for c in range(4):
                        dve.wait_ge(sem("htok_hi"), c + 1)
                        tt(hlo[:, 2 * c:2 * c + 2, :], ps[:, 6 * (c % 2):6 * (c % 2) + 2, :],
                           hhi[:, 2 * c:2 * c + 2, :].bitcast(F32), ALU.subtract).then_inc(sem("htok_lo"), 1)
                    dve.wait_ge(sem("ranks_done"), 1)
                    cnt, nblk, incl, base = (rt[:, 8 * q:8 * q + 8] for q in range(4))
                    link(dve.tensor_copy(cnt, ps[:, 5, 0:NE]))
                    link(dve.tensor_scalar(nblk, cnt, 0.0, None, ALU.is_gt))
                    for q in range(1, 4):
                        link(stt(nblk, cnt, float(q * P), nblk, ALU.is_gt, ALU.add))
                    link(dve.tensor_tensor_scan(incl, C("ones")[:, 0:NE], nblk, 0.0, ALU.mult, ALU.add))
                    link(tt(base, incl, nblk, ALU.subtract))
                    link(dve.tensor_scalar(base, base, float(P), None, ALU.mult))
                    link(tt(slot(6), ps[:, 4, 0:32].rearrange("p (t e) -> p t e", t=4),
                            base.unsqueeze(1).broadcast_to([P, 4, NE]), ALU.add))
                    for hot, q in ((3, 4), (5, 5)):
                        link(tt(slot(1), slot(hot), slot(6)))
                        link(dve.tensor_reduce(four(q), slot(1), AX.X, ALU.add))
                    eb3 = junk[:, 0:128].rearrange("p (b e) -> p b e", b=16)
                    link(tt(eb3, incl.unsqueeze(1).broadcast_to([P, 16, NE]),
                            C("blocks").rearrange("p (b e) -> p b e", b=16), ALU.is_le))
                    link(dve.tensor_reduce(rt[:, 40:56], eb3, AX.X, ALU.add))
                    link(dve.tensor_scalar(rt[:, 40:56], rt[:, 40:56], float(NE - 1), None, ALU.min))
                    mark(dve.tensor_copy(ebi[:], rt[:, 40:56]), "eb_ready")
                    dve.wait_ge(sem("route_exp"), 1)
                    link(dve.tensor_scalar(four(3), four(2), 1.0, None, ALU.add))
                    link(dve.reciprocal(four(3), four(3)))
                    link(tt(four(2), four(2), four(3)))
                    diag = junk[:].rearrange("p (c j) -> p c j", c=4)
                    ident3 = C("ident").unsqueeze(1).broadcast_to([P, 4, P])

                    def along(ap4):
                        return ap4.unsqueeze(2).broadcast_to([P, 4, P])

                    for q, src in enumerate((4, 5, 3, 2)):
                        if q:
                            dve.wait_ge(sem("bc_done"), q)
                        mark(tt(diag, ident3, along(four(src))), "diag_ready")
                    dve.wait_ge(sem("bc_done"), 4)
                    dve.wait_ge(sem("bc_ready"), 4)
                    jcol, pslot = rt[:, 56:57], rt[:, 80:81]
                    link(dve.tensor_copy(jcol, C("part")))
                    dve.memset(yh[:].bitcast(I32), 0).then_inc(sem("zeroed"), 1)
                    dve.memset(SC[:].bitcast(I32), 0).then_inc(sem("SC_ready"), 1)
                    dve.memset(yl[:].bitcast(I32), 0).then_inc(sem("y_ready"), 1)
                    iota3 = C("iota").unsqueeze(1).broadcast_to([P, 4, P])
                    j4 = junk[:].rearrange("p (c j) -> p c j", c=4)
                    PER = 9
                    local = [0]

                    def step(ins, b):
                        local[0] += 1
                        ins.then_inc(sem("block_step"), 1)
                        dve.wait_ge(sem("block_step"), PER * b + local[0])

                    def token_to_slot(link):
                        link(tt(G[:], along(four(4)), iota3, ALU.is_equal))
                        link(tt(j4, along(four(5)), iota3, ALU.is_equal))
                        tt(G[:], G[:].bitcast(F32), j4, ALU.add).then_inc(sem("G_ready"), 1)
                        link(dve.tensor_scalar(small[:, 220:228], small[:, 220:228], -float(P), None, ALU.add))

                    def slot_to_token(link):
                        link(stt(junk[:], bc[:, 0, :], jcol, bc[:, 2, :], ALU.is_equal, ALU.mult))
                        link(dve.tensor_reduce(rt[:, 81:82], junk[:], AX.X, ALU.add))
                        link(stt(junk[:], bc[:, 1, :], jcol, bc[:, 3, :], ALU.is_equal, ALU.mult))
                        link(dve.tensor_reduce(rt[:, 82:83], junk[:], AX.X, ALU.add))
                        tt(pslot, rt[:, 81:82], rt[:, 82:83], ALU.add).then_inc(sem("pslot_ready"), 1)
                        link(dve.tensor_scalar(junk[:], bc[:, 0, :], jcol, None, ALU.is_equal))
                        link(stt(SC[:], bc[:, 1, :], jcol, junk[:], ALU.is_equal, ALU.add))
                        dve.tensor_scalar(jcol, jcol, float(P), None, ALU.add).then_inc(sem("SC_ready"), 1)

                    def low(b, t):
                        if t % 3 != 2:
                            dve.wait_ge(sem("him_ready"), NT * b + t + 1)
                            tt(wlm[:, t % 4, :], rawm_tile(t), whm[:, t % 4, :].bitcast(F32), ALU.subtract)\
                                .then_inc(sem("lom_dve"), 1)

                    def tokens(b):
                        dve.wait_ge(sem("gather_done"), 2 * b + 2)
                        dve.tensor_copy(xgl[:], ps[:, 2:4, :].rearrange("p b (k s) -> p (b k) s", s=P))\
                            .then_inc(sem("xgl_ready"), 1)

                    def add(n, b):
                        dve.wait_ge(sem("scatter_done"), DC * b + n + 1)
                        dve.wait_ge(sem("xm_done"), DC * b + n + 1)
                        stt(x[:, n, :], ps[:, 4 + n % 4, :], mod[:, 88 + n:89 + n], x[:, n, :]).then_inc(sem("xm_done"), 1)

                    def times(b, half):
                        dve.wait_ge(sem("tilem_done"), NT * b + 8 * half + 12)
                        dve.wait_ge(sem("sgm_ready"), 2 * b + half + 1)
                        tt(tm[:, half, :], sgm[:, half, :], ps[:, 2 * half + 1, :]).then_inc(sem("tm_ready"), 1)

                    def hidden(b, half):
                        dve.wait_ge(sem("hih_ready"), 2 * b + half + 1)
                        tt(hil[:, 4 * half:4 * half + 4, :], ps[:, 4 + half, :].rearrange("p (k s) -> p k s", s=P),
                           hih[:, 4 * half:4 * half + 4, :].bitcast(F32), ALU.subtract).then_inc(sem("hil_ready"), 1)

                    token_to_slot(link)
                    for t in range(4):
                        low(0, t)
                    tokens(0)
                    with dve.Fori(0, NB) as b:
                        for t in range(NT):
                            if t + 4 < NT:
                                low(b, t + 4)
                            else:
                                low(b + 1, t + 4 - NT)
                            if t == 3:
                                for n in range(4):
                                    add(n, b)
                            if t == 7:
                                times(b, 0)
                                for n in range(4, DC):
                                    add(n, b)
                            if t == 9:
                                slot_to_token(lambda ins: step(ins, b))
                            if t == 11:
                                hidden(b, 0)
                            if t == 13:
                                token_to_slot(lambda ins: step(ins, b))
                            if t == 15:
                                times(b, 1)
                            if t == 19:
                                hidden(b, 1)
                                tokens(b + 1)
                            if t == 23:
                                dve.wait_ge(sem("yh_ready"), b + 1)
                                stt(yl[:], ps[:, 6:8, :].rearrange("p b n -> p (b n)"), pslot, yh[:].bitcast(F32),
                                    ALU.mult, ALU.subtract).then_inc(sem("y_ready"), 1)
                    assert local[0] == PER, local
                    for n in range(DC):
                        add(n, NB)
                    dve.wait_ge(sem("xm_done"), DC * (NB + 2))
            norm(4)


def _chunks(a):
    return a.reshape((-1, P) + a.shape[1:]).swapaxes(0, 1)


def _tiles(w):
    k, n = w.shape
    return w.reshape(k // P, P, n // P, P).transpose(2, 1, 0, 3).reshape(n // P, P, k)


def kernel(**inputs):
    import concourse.bacc as _bacc
    from concourse.bass_utils import run_bass_kernel_spmd as _run

    a = {k: np.asarray(v) for k, v in inputs.items()}
    q_cols = np.concatenate([np.r_[c * 64:c * 64 + 64, (c + 4) * 64:(c + 4) * 64 + 64] for c in range(4)])
    db0 = 512 + 256 + 768
    in_cols = np.concatenate([q_cols, np.arange(512, db0), np.arange(db0 + 8, 2312)])
    out_rows = np.concatenate([q_cols, np.arange(512, 1024)])

    tiles = []
    for layer in range(DEPTH):
        tiles.append(_tiles(a["w_in"][layer][:, in_cols]))
        tiles.append(_tiles(a["w_out"][layer][out_rows]))
        if layer == 0:
            g, u = _tiles(a["ffn_w_gate"][0]), _tiles(a["ffn_w_up"][0])
            tiles.append(np.stack([g, u], 1).reshape(-1, P, D))
    tiles.append(np.zeros((2, P, D), np.float32))
    w8 = np.concatenate(tiles)
    which = {"g": a["moe_w_gate"][0], "u": a["moe_w_up"][0], "d": a["moe_w_down"][0]}
    wm = np.stack([which[m][:, k * P:(k + 4) * P, f * S:(f + 1) * S].reshape(NE, 4, P, S).transpose(0, 2, 1, 3)
                   for m, f, k in UNITS], 1).reshape(NE * NUN, P, 4 * S)
    wd = _tiles(a["ffn_w_down"][0]).reshape(DC, P, 2, KD * P)
    w11 = wd.transpose(0, 2, 1, 3).reshape(2 * DC, P, KD * P)

    ada = a["ada_w"].reshape(4, DC, P, 12, 256).transpose(0, 3, 2, 1, 4).reshape(48, P, DC * 256)

    params = np.zeros((P, N_PAR), np.float32)

    def put(name, v):
        lo, hi = P_COLS[name]
        params[:v.shape[0], lo:hi] = v.reshape(v.shape[0], hi - lo)

    put("adab", _chunks(a["ada_b"].reshape(-1)))
    put("ng", _chunks(np.stack([a["norm_mix_g"], a["norm_ffn_g"]], 1).reshape(-1)))
    put("fg", _chunks(a["final_norm_g"]))
    put("c", _chunks(a["c"][0]))
    put("wba", a["w_in"][:, :, db0:db0 + 8].reshape(DEPTH, DC, P, 8).transpose(2, 0, 1, 3))
    for name, key in (("dtb", "dn_dt_bias"), ("alog", "dn_a_log")):
        lo, hi = P_COLS[name]
        params[4:8, lo:hi] = a[key].T
    put("sink", np.broadcast_to(a["attn_sinks"].reshape(1, -1), (P, DEPTH * 8)))
    put("dconv", a["dn_conv_w"].reshape(DEPTH, DN_CONV, 6, P).transpose(3, 0, 2, 1))
    put("dng", np.tile(a["dn_norm_g"].T, (2, 1)))
    put("cconv", a["cv_dw_w"].reshape(DEPTH, CV_K, 2, P).transpose(3, 0, 2, 1))
    for name, key in (("cb", "cv_dw_b"), ("lng", "cv_ln_g"), ("lnb", "cv_ln_b")):
        put(name, a[key].reshape(DEPTH, 2, P).transpose(2, 0, 1))
    put("rw", a["router_w"][0].reshape(DC, P, NE).transpose(1, 0, 2))
    put("rb", np.broadcast_to(a["router_b"], (P, NE)))

    arrays = {
        "xT": a["x"][0].T, "consts": constants(), "params": params, "pos": a["positions"],
        "ada": ada, "w8": w8, "w11": w11, "wm": wm,
    }
    nc = _bacc.Bacc("TRN2", target_bir_lowering=False, num_devices=1)
    arrays = {k: np.ascontiguousarray(v) for k, v in arrays.items()}
    args = [nc.dram_tensor(f"in_{k}", v.shape, mybir.dt.from_np(v.dtype), kind="ExternalInput").ap()
            for k, v in arrays.items()]
    out = nc.dram_tensor("out_T", (D, S), F32, kind="ExternalOutput").ap()
    trunk(nc, *args, out)
    r = _run(nc, [{f"in_{k}": v for k, v in arrays.items()}], core_ids=[0])
    return np.ascontiguousarray(r.results[0]["out_T"].T)[None]
```
